# Optimizing a Trainium2 kernel written in Bass

```python
import jax, jax.numpy as jnp
from jax import lax
import numpy as np
import math

D_MODEL = 1024
BATCH = 1
SEQ = 512
DEPTH = 2

GRID_W = 64
CTX_LEN = 256
N_EVEN = (DEPTH + 1) // 2
N_ODD = DEPTH // 2

MLA_HEADS = 8
MLA_Q_RANK = 384
MLA_KV_RANK = 256
MLA_NOPE = 64
MLA_ROPE = 32
MLA_V = 64
MLA_QK = MLA_NOPE + MLA_ROPE
GQA_HEADS = 8
GQA_KV_HEADS = 2
GQA_DIM = 64
EVEN_SPLITS = (MLA_Q_RANK, MLA_KV_RANK, MLA_ROPE, GQA_HEADS * GQA_DIM,
               GQA_KV_HEADS * GQA_DIM, GQA_KV_HEADS * GQA_DIM)
EVEN_IN = sum(EVEN_SPLITS)
EVEN_MIX = MLA_HEADS * MLA_V + GQA_HEADS * GQA_DIM
MLSTM_HEADS = 8
MLSTM_QK = 64
MLSTM_V = 128
MLSTM_CONV = 3
MLSTM_CHUNK = 64
ODD_SPLITS = (2 * MLSTM_HEADS * MLSTM_QK, MLSTM_HEADS * MLSTM_V, MLSTM_HEADS * MLSTM_V, 4 * MLSTM_HEADS)
ODD_IN = sum(ODD_SPLITS)
D_FF = 2816
FFN_CONV = 3

Q_BLOCK = 128
ROPE_THETA = 10000.0
EPS = 1e-6


def rmsnorm(x, g):
    xf = x.astype(jnp.float32)
    y = xf * lax.rsqrt(jnp.mean(xf * xf, axis=-1, keepdims=True) + EPS)
    return (y * g.astype(jnp.float32)).astype(x.dtype)

def modulate(h, shift, scale):
    return h * (1 + scale) + shift

def split_cols(p, sizes):
    return jnp.split(p, np.cumsum(sizes)[:-1].tolist(), axis=-1)

def dwconv(x, w, b):
    width, T = w.shape[0], x.shape[1]
    left = (width - 1) // 2
    xp = jnp.pad(x, ((0, 0), (left, width - 1 - left), (0, 0)))
    return sum(xp[:, j:j + T] * w[j] for j in range(width)) + b

def axial_rope_tables(n_tokens, rot_dim):
    rows = n_tokens // GRID_W
    row = jnp.repeat(jnp.arange(rows), GRID_W).astype(jnp.float32)
    col = jnp.tile(jnp.arange(GRID_W), rows).astype(jnp.float32)
    n_freq = rot_dim // 4
    inv = ROPE_THETA ** (-jnp.arange(n_freq, dtype=jnp.float32) / n_freq)
    a_r, a_c = row[:, None] * inv, col[:, None] * inv
    ang = jnp.concatenate([a_r, a_r, a_c, a_c], axis=-1)
    return jnp.cos(ang), jnp.sin(ang)

def apply_rope(x, cos, sin):
    a1, a2, b1, b2 = jnp.split(x, 4, axis=-1)
    rot = jnp.concatenate([-a2, a1, -b2, b1], axis=-1)
    shape = (1, x.shape[1]) + (1,) * (x.ndim - 3) + (x.shape[-1],)
    return x * cos.reshape(shape).astype(x.dtype) + rot * sin.reshape(shape).astype(x.dtype)

def attend(q, k, v):
    B, T, G, R, dk = q.shape
    nb = T // Q_BLOCK
    scale = dk ** -0.5
    qb = jnp.moveaxis(q.reshape(B, nb, Q_BLOCK, G, R, dk), 1, 0)

    def block(qi):
        s = jnp.einsum('bqgrd,bsgd->bgrqs', qi, k).astype(jnp.float32) * scale
        p = jax.nn.softmax(s, axis=-1).astype(v.dtype)
        return jnp.einsum('bgrqs,bsgd->bqgrd', p, v)

    out = lax.map(block, qb)
    return jnp.moveaxis(out, 0, 1).reshape(B, T, G, R, v.shape[-1])

def mla_q(cq, g_qa, w_qb, g_q, rope):
    B, T, _ = cq.shape
    q = jnp.dot(rmsnorm(cq, g_qa), w_qb).reshape(B, T, MLA_HEADS, MLA_QK)
    q = rmsnorm(q, g_q)
    if rope is not None:
        q = jnp.concatenate([q[..., :MLA_NOPE], apply_rope(q[..., MLA_NOPE:], *rope)], axis=-1)
    return q[:, :, :, None, :]

def mla_kv(ckv, k_rope, g_kva, w_kvb, g_k, rope):
    B, T, _ = ckv.shape
    kv = jnp.dot(rmsnorm(ckv, g_kva), w_kvb).reshape(B, T, MLA_HEADS, MLA_NOPE + MLA_V)
    k_nope, v = kv[..., :MLA_NOPE], kv[..., MLA_NOPE:]
    k_pe = jnp.broadcast_to(k_rope[:, :, None, :], (B, T, MLA_HEADS, MLA_ROPE))
    k = rmsnorm(jnp.concatenate([k_nope, k_pe], axis=-1), g_k)
    if rope is not None:
        k = jnp.concatenate([k[..., :MLA_NOPE], apply_rope(k[..., MLA_NOPE:], *rope)], axis=-1)
    return k, v

def gqa_q(q, g_q, rope):
    B, T, _ = q.shape
    q = rmsnorm(q.reshape(B, T, GQA_HEADS, GQA_DIM), g_q)
    if rope is not None:
        q = apply_rope(q, *rope)
    return q.reshape(B, T, GQA_KV_HEADS, GQA_HEADS // GQA_KV_HEADS, GQA_DIM)

def gqa_kv(k, v, g_k, rope):
    B, T, _ = k.shape
    k = rmsnorm(k.reshape(B, T, GQA_KV_HEADS, GQA_DIM), g_k)
    if rope is not None:
        k = apply_rope(k, *rope)
    return k, v.reshape(B, T, GQA_KV_HEADS, GQA_DIM)

def even_mixer(h_lat, h_ctx, w_in, g_qa, w_qb, g_kva, w_kvb, g_mq, g_mk, g_gq, g_gk, w_out,
               rope_mla, rope_gqa, need_ctx_out):
    cq_l, ckv_l, kr_l, gq_l, gk_l, gv_l = split_cols(jnp.dot(h_lat, w_in), EVEN_SPLITS)
    cq_c, ckv_c, kr_c, gq_c, gk_c, gv_c = split_cols(jnp.dot(h_ctx, w_in), EVEN_SPLITS)
    ka_c, va_c = mla_kv(ckv_c, kr_c, g_kva, w_kvb, g_mk, None)
    ka_l, va_l = mla_kv(ckv_l, kr_l, g_kva, w_kvb, g_mk, rope_mla)
    kb_c, vb_c = gqa_kv(gk_c, gv_c, g_gk, None)
    kb_l, vb_l = gqa_kv(gk_l, gv_l, g_gk, rope_gqa)
    ka, va = jnp.concatenate([ka_c, ka_l], axis=1), jnp.concatenate([va_c, va_l], axis=1)
    kb, vb = jnp.concatenate([kb_c, kb_l], axis=1), jnp.concatenate([vb_c, vb_l], axis=1)

    def merge(o_a, o_b):
        B, T = o_a.shape[:2]
        return jnp.dot(jnp.concatenate([o_a.reshape(B, T, -1), o_b.reshape(B, T, -1)], axis=-1), w_out)

    out_lat = merge(attend(mla_q(cq_l, g_qa, w_qb, g_mq, rope_mla), ka, va),
                    attend(gqa_q(gq_l, g_gq, rope_gqa), kb, vb))
    out_ctx = None
    if need_ctx_out:
        out_ctx = merge(attend(mla_q(cq_c, g_qa, w_qb, g_mq, None), ka_c, va_c),
                        attend(gqa_q(gq_c, g_gq, None), kb_c, vb_c))
    return out_lat, out_ctx

def mlstm_inputs(h, w_in, conv_w, conv_b, gate_b):
    B, T, _ = h.shape
    qk, v, o, g = split_cols(jnp.dot(h, w_in), ODD_SPLITS)
    q, k = jnp.split(jax.nn.silu(dwconv(qk, conv_w, conv_b)), 2, axis=-1)

    def heads(t, d):
        return jnp.swapaxes(t.reshape(B, T, MLSTM_HEADS, d), 1, 2).astype(jnp.float32)

    g = (g + gate_b).astype(jnp.float32).reshape(B, T, 4, MLSTM_HEADS)
    g = jnp.transpose(g, (2, 0, 3, 1))
    gates = (g[0], jax.nn.log_sigmoid(g[1]), g[2], jax.nn.log_sigmoid(g[3]))
    return heads(q, MLSTM_QK), heads(k, MLSTM_QK) * MLSTM_QK ** -0.5, heads(v, MLSTM_V), o, gates

def mlstm_state_update(state, k, v, log_i, b):
    C, n, m = state
    b_last = b[..., -1]
    a = b_last[..., None] - b + log_i
    m_new = jnp.maximum(b_last + m, jnp.max(a, axis=-1))
    decay = jnp.exp(b_last + m - m_new)
    w = jnp.exp(a - m_new[..., None])
    C_new = decay[..., None, None] * C + jnp.einsum('bhs,bhsv,bhsd->bhvd', w, v, k)
    n_new = decay[..., None] * n + jnp.einsum('bhs,bhsd->bhd', w, k)
    return (C_new, n_new, m_new)

def mlstm_chunkwise(q, k, v, log_i, log_f, state0):
    B, H, T, dk = q.shape
    dv = v.shape[-1]
    L = MLSTM_CHUNK
    nc = T // L
    lower = jnp.tril(jnp.ones((L, L), dtype=bool))

    def chunks(t):
        return jnp.moveaxis(t.reshape((B, H, nc, L) + t.shape[3:]), 2, 0)

    def step(state, inp):
        C, n, m = state
        qc, kc, vc, ic, fc = inp
        b = jnp.cumsum(fc, axis=-1)
        logw = jnp.where(lower, b[..., :, None] - b[..., None, :] + ic[..., None, :], -jnp.inf)
        log_inter = b + m[..., None]
        m_t = jnp.maximum(log_inter, jnp.max(logw, axis=-1))
        w_inter = jnp.exp(log_inter - m_t)
        s = jnp.einsum('bhtd,bhsd->bhts', qc, kc) * jnp.exp(logw - m_t[..., None])
        num = w_inter[..., None] * jnp.einsum('bhvd,bhtd->bhtv', C, qc) + jnp.einsum('bhts,bhsv->bhtv', s, vc)
        den = w_inter * jnp.einsum('bhd,bhtd->bht', n, qc) + jnp.sum(s, axis=-1)
        h = num / jnp.maximum(jnp.abs(den), jnp.exp(-m_t))[..., None]
        return mlstm_state_update(state, kc, vc, ic, b), h

    state, h = lax.scan(step, state0, (chunks(q), chunks(k), chunks(v), chunks(log_i), chunks(log_f)))
    return jnp.moveaxis(h, 0, 2).reshape(B, H, T, dv), state

def mlstm_direction(q_l, k_l, v_l, li_l, lf_l, q_c, k_c, v_c, li_c, lf_c, need_ctx_out):
    B, H = q_l.shape[:2]
    state0 = (jnp.zeros((B, H, MLSTM_V, MLSTM_QK), jnp.float32),
              jnp.zeros((B, H, MLSTM_QK), jnp.float32),
              jnp.zeros((B, H), jnp.float32))
    if need_ctx_out:
        h_c, state_c = mlstm_chunkwise(q_c, k_c, v_c, li_c, lf_c, state0)
    else:
        h_c = None
        state_c = mlstm_state_update(state0, k_c, v_c, li_c, jnp.cumsum(lf_c, axis=-1))
    h_l, _ = mlstm_chunkwise(q_l, k_l, v_l, li_l, lf_l, state_c)
    return h_l, h_c

def odd_mixer(h_lat, h_ctx, w_in, conv_w, conv_b, gate_b, out_g, w_out, need_ctx_out):
    q_l, k_l, v_l, o_l, g_l = mlstm_inputs(h_lat, w_in, conv_w, conv_b, gate_b)
    q_c, k_c, v_c, o_c, g_c = mlstm_inputs(h_ctx, w_in, conv_w, conv_b, gate_b)

    def rev(t):
        return jnp.flip(t, axis=2)

    hf_l, hf_c = mlstm_direction(q_l, k_l, v_l, g_l[0], g_l[1], q_c, k_c, v_c, g_c[0], g_c[1], need_ctx_out)
    hb_l, hb_c = mlstm_direction(rev(q_l), rev(k_l), rev(v_l), rev(g_l[2]), rev(g_l[3]),
                                 rev(q_c), rev(k_c), rev(v_c), rev(g_c[2]), rev(g_c[3]), need_ctx_out)

    def readout(hf, hb, o):
        h = jnp.swapaxes(hf + rev(hb), 1, 2)
        B, T = h.shape[:2]
        h = rmsnorm(h, out_g).reshape(B, T, -1).astype(o.dtype)
        return jnp.dot(h * jax.nn.sigmoid(o), w_out)

    out_lat = readout(hf_l, hb_l, o_l)
    out_ctx = readout(hf_c, hb_c, o_c) if need_ctx_out else None
    return out_lat, out_ctx

def conv_ffn(h, w_up, conv_w, conv_b, w_down):
    gate, val = jnp.split(jnp.dot(h, w_up), 2, axis=-1)
    return jnp.dot(jax.nn.silu(dwconv(gate, conv_w, conv_b)) * val, w_down)

def first_inputs(seed: int = 0) -> dict:
    key = jax.random.key(seed)
    keys = jax.random.split(key, 40)
    counter = iter(range(40))
    D = D_MODEL

    def nrm(shape, scale):
        return jax.random.normal(keys[next(counter)], shape, jnp.float32) * scale

    def gain(shape):
        return 1.0 + nrm(shape, 0.05)

    H = MLSTM_HEADS
    i_bias = nrm((N_ODD, 2, 1, H), 0.1)
    f_bias = jnp.linspace(3.0, 6.0, H, dtype=jnp.float32) + nrm((N_ODD, 2, 1, H), 0.1)
    ml_gate_b = jnp.concatenate([i_bias, f_bias], axis=2).reshape(N_ODD, 4 * H)
    return {
        'x': nrm((BATCH, SEQ, D), 1.0),
        'c': nrm((BATCH, D), 1.0),
        'ctx': nrm((BATCH, CTX_LEN, D), 1.0),
        'c_ctx': nrm((D,), 1.0),
        'ada_w': nrm((DEPTH, D, 6 * D), 0.5 * D ** -0.5),
        'ada_b': nrm((DEPTH, 6 * D), 0.02),
        'norm1_g': gain((DEPTH, D)),
        'norm2_g': gain((DEPTH, D)),
        'ffn_w_up': nrm((DEPTH, D, 2 * D_FF), D ** -0.5),
        'ffn_conv_w': nrm((DEPTH, FFN_CONV, D_FF), 0.5),
        'ffn_conv_b': nrm((DEPTH, D_FF), 0.02),
        'ffn_w_down': nrm((DEPTH, D_FF, D), D_FF ** -0.5),
        'att_w_in': nrm((N_EVEN, D, EVEN_IN), D ** -0.5),
        'mla_qa_g': gain((N_EVEN, MLA_Q_RANK)),
        'mla_w_qb': nrm((N_EVEN, MLA_Q_RANK, MLA_HEADS * MLA_QK), MLA_Q_RANK ** -0.5),
        'mla_kva_g': gain((N_EVEN, MLA_KV_RANK)),
        'mla_w_kvb': nrm((N_EVEN, MLA_KV_RANK, MLA_HEADS * (MLA_NOPE + MLA_V)), MLA_KV_RANK ** -0.5),
        'mla_q_g': gain((N_EVEN, MLA_QK)),
        'mla_k_g': gain((N_EVEN, MLA_QK)),
        'gqa_q_g': gain((N_EVEN, GQA_DIM)),
        'gqa_k_g': gain((N_EVEN, GQA_DIM)),
        'att_w_out': nrm((N_EVEN, EVEN_MIX, D), EVEN_MIX ** -0.5),
        'ml_w_in': nrm((N_ODD, D, ODD_IN), D ** -0.5),
        'ml_conv_w': nrm((N_ODD, MLSTM_CONV, 2 * H * MLSTM_QK), 0.5),
        'ml_conv_b': nrm((N_ODD, 2 * H * MLSTM_QK), 0.02),
        'ml_gate_b': ml_gate_b,
        'ml_out_g': gain((N_ODD, H, MLSTM_V)),
        'ml_w_out': nrm((N_ODD, H * MLSTM_V, D), (H * MLSTM_V) ** -0.5),
    }

def first_block(x, c, ctx, c_ctx, ada_w, ada_b, norm1_g, norm2_g, ffn_w_up, ffn_conv_w, ffn_conv_b,
              ffn_w_down, att_w_in, mla_qa_g, mla_w_qb, mla_kva_g, mla_w_kvb, mla_q_g, mla_k_g,
              gqa_q_g, gqa_k_g, att_w_out, ml_w_in, ml_conv_w, ml_conv_b, ml_gate_b, ml_out_g, ml_w_out):
    n_lat = x.shape[1]
    rope_mla = axial_rope_tables(n_lat, MLA_ROPE)
    rope_gqa = axial_rope_tables(n_lat, GQA_DIM)
    for layer in range(DEPTH):
        need_ctx_out = layer < DEPTH - 1
        j = layer // 2
        mod_lat = (jnp.dot(jax.nn.silu(c), ada_w[layer]) + ada_b[layer])[:, None, :]
        mod_ctx = jnp.dot(jax.nn.silu(c_ctx), ada_w[layer]) + ada_b[layer]
        sh1, sc1, gt1, sh2, sc2, gt2 = jnp.split(mod_lat, 6, axis=-1)
        csh1, csc1, cgt1, csh2, csc2, cgt2 = jnp.split(mod_ctx, 6, axis=-1)
        h_lat = modulate(rmsnorm(x, norm1_g[layer]), sh1, sc1)
        h_ctx = modulate(rmsnorm(ctx, norm1_g[layer]), csh1, csc1)
        if layer % 2 == 0:
            out_lat, out_ctx = even_mixer(h_lat, h_ctx, att_w_in[j], mla_qa_g[j], mla_w_qb[j], mla_kva_g[j],
                                          mla_w_kvb[j], mla_q_g[j], mla_k_g[j], gqa_q_g[j], gqa_k_g[j],
                                          att_w_out[j], rope_mla, rope_gqa, need_ctx_out)
        else:
            out_lat, out_ctx = odd_mixer(h_lat, h_ctx, ml_w_in[j], ml_conv_w[j], ml_conv_b[j], ml_gate_b[j],
                                         ml_out_g[j], ml_w_out[j], need_ctx_out)
        x = x + gt1 * out_lat
        x = x + gt2 * conv_ffn(modulate(rmsnorm(x, norm2_g[layer]), sh2, sc2),
                               ffn_w_up[layer], ffn_conv_w[layer], ffn_conv_b[layer], ffn_w_down[layer])
        if need_ctx_out:
            ctx = ctx + cgt1 * out_ctx
            ctx = ctx + cgt2 * conv_ffn(modulate(rmsnorm(ctx, norm2_g[layer]), csh2, csc2),
                                       ffn_w_up[layer], ffn_conv_w[layer], ffn_conv_b[layer], ffn_w_down[layer])
    return x


CHUNK = 64
N_A_LAYERS = DEPTH // 2
N_B_LAYERS = DEPTH - N_A_LAYERS
D_RNN = D_MODEL
N_LRU_BLOCKS = 8
LRU_BLOCK = D_RNN // N_LRU_BLOCKS
CONV_WIDTH = 4
LRU_C = 8.0
N_HEADS = 8
HEAD_DIM = D_MODEL // (2 * N_HEADS)
SUBLN_EPS = 1e-5


def rmsnorm_2(x, g, eps=EPS):
    xf = x.astype(jnp.float32)
    y = xf * lax.rsqrt(jnp.mean(xf * xf, axis=-1, keepdims=True) + eps)
    return (y * g.astype(jnp.float32)).astype(x.dtype)

def swiglu(h, w_gate, w_up, w_down):
    return (jax.nn.silu(h @ w_gate) * (h @ w_up)) @ w_down

def causal_depthwise_conv(x, w, b):
    S = x.shape[1]
    xp = jnp.pad(x, ((0, 0), (CONV_WIDTH - 1, 0), (0, 0)))
    out = b
    for k in range(CONV_WIDTH):
        out = out + xp[:, k:k + S, :] * w[k]
    return out

def _lru_combine(c1, c2):
    a1, b1 = c1
    a2, b2 = c2
    return a1 * a2, a2 * b1 + b2

def rg_lru(x, w_a, b_a, w_x, b_x, lam):
    B, S, _ = x.shape
    xb = x.reshape(B, S, N_LRU_BLOCKS, LRU_BLOCK)
    gate_a = jnp.einsum('bsnh,nhk->bsnk', xb, w_a).reshape(B, S, D_RNN) + b_a
    gate_x = jnp.einsum('bsnh,nhk->bsnk', xb, w_x).reshape(B, S, D_RNN) + b_x
    r = jax.nn.sigmoid(gate_a.astype(jnp.float32))
    i = jax.nn.sigmoid(gate_x.astype(jnp.float32))
    log_a = -LRU_C * r * jax.nn.softplus(-lam.astype(jnp.float32))
    a = jnp.exp(log_a)
    mult = jnp.sqrt(-jnp.expm1(2.0 * log_a))
    bx = mult * (i * x.astype(jnp.float32))
    _, h = lax.associative_scan(_lru_combine, (a, bx), axis=1)
    return h.astype(x.dtype)

def recurrent_block(h, w_in, conv_w, conv_b, w_a, b_a, w_x, b_x, lam, w_out):
    proj = h @ w_in
    gate, rec = proj[..., :D_RNN], proj[..., D_RNN:]
    rec = causal_depthwise_conv(rec, conv_w, conv_b)
    rec = rg_lru(rec, w_a, b_a, w_x, b_x, lam)
    return (jax.nn.gelu(gate) * rec) @ w_out

def rope_tables(S):
    pos = jnp.arange(S, dtype=jnp.float32)
    inv_freq = ROPE_THETA ** (-jnp.arange(0, HEAD_DIM, 2, dtype=jnp.float32) / HEAD_DIM)
    ang = pos[:, None] * inv_freq[None, :]
    ang = jnp.concatenate([ang, ang], axis=-1)
    return jnp.cos(ang), jnp.sin(ang)

def apply_rope_2(t, cos, sin):
    tf = t.astype(jnp.float32)
    half = HEAD_DIM // 2
    rot = jnp.concatenate([-tf[..., half:], tf[..., :half]], axis=-1)
    c = cos[None, :, None, None, :]
    s = sin[None, :, None, None, :]
    return (tf * c + rot * s).astype(t.dtype)

def shared_kv(x, kv_norm, w_k, w_v, k_norm, cos, sin):
    B, S, _ = x.shape
    h = rmsnorm_2(x, kv_norm)
    k = (h @ w_k).reshape(B, S, N_HEADS, 2, HEAD_DIM)
    k = apply_rope_2(rmsnorm_2(k, k_norm), cos, sin)
    k = k.transpose(0, 2, 3, 1, 4)
    v = (h @ w_v).reshape(B, S, N_HEADS, 2 * HEAD_DIM).transpose(0, 2, 1, 3)
    return k, v

def diff_attention(h, k, v, w_q, q_norm, lq1, lq2, lk1, lk2, sub_norm, w_o, cos, sin, lambda_init):
    B, S, _ = h.shape
    nb = S // Q_BLOCK
    q = (h @ w_q).reshape(B, S, N_HEADS, 2, HEAD_DIM)
    q = apply_rope_2(rmsnorm_2(q, q_norm), cos, sin) * (HEAD_DIM ** -0.5)
    q_blocks = q.reshape(B, nb, Q_BLOCK, N_HEADS, 2, HEAD_DIM).transpose(1, 0, 3, 4, 2, 5)
    lam = (jnp.exp(jnp.sum((lq1 * lk1).astype(jnp.float32)))
           - jnp.exp(jnp.sum((lq2 * lk2).astype(jnp.float32))) + lambda_init)
    key_chunk = jnp.arange(S) // CHUNK
    vf = v.astype(jnp.float32)

    def one_block(args):
        qb, bi = args
        scores = jnp.einsum('bhcqd,bhckd->bhcqk', qb, k, preferred_element_type=jnp.float32)
        q_chunk = (bi * Q_BLOCK + jnp.arange(Q_BLOCK)) // CHUNK
        mask = key_chunk[None, :] <= q_chunk[:, None]
        p = jax.nn.softmax(jnp.where(mask, scores, -jnp.inf), axis=-1)
        attn = p[:, :, 0] - lam * p[:, :, 1]
        return jnp.einsum('bhqk,bhkd->bhqd', attn, vf)

    o = lax.map(one_block, (q_blocks, jnp.arange(nb)))
    o = o.transpose(1, 0, 3, 2, 4).reshape(B, S, N_HEADS, 2 * HEAD_DIM)
    o = rmsnorm_2(o, sub_norm, SUBLN_EPS) * (1.0 - lambda_init)
    return o.reshape(B, S, D_MODEL).astype(h.dtype) @ w_o

def second_inputs(seed: int = 0) -> dict:
    key = jax.random.key(seed)
    ks = iter(jax.random.split(key, 64))
    f32 = jnp.float32

    def dense(shape, fan_in):
        return jax.random.normal(next(ks), shape, f32) * (fan_in ** -0.5)

    def gain(shape):
        return 1.0 + 0.02 * jax.random.normal(next(ks), shape, f32)

    def bias(shape):
        return 0.01 * jax.random.normal(next(ks), shape, f32)

    nA, nB = N_A_LAYERS, N_B_LAYERS
    u = jax.random.uniform(next(ks), (nA, D_RNN), f32, 0.9, 0.999)
    a0 = u ** (1.0 / LRU_C)
    rec_lambda = jnp.log(a0) - jnp.log1p(-a0)
    return {
        'x': jax.random.normal(next(ks), (BATCH, SEQ, D_MODEL), f32),
        'ffn1_norm': gain((DEPTH, D_MODEL)),
        'ffn1_w_gate': dense((DEPTH, D_MODEL, D_FF), D_MODEL),
        'ffn1_w_up': dense((DEPTH, D_MODEL, D_FF), D_MODEL),
        'ffn1_w_down': dense((DEPTH, D_FF, D_MODEL), D_FF),
        'ffn2_norm': gain((DEPTH, D_MODEL)),
        'ffn2_w_gate': dense((DEPTH, D_MODEL, D_FF), D_MODEL),
        'ffn2_w_up': dense((DEPTH, D_MODEL, D_FF), D_MODEL),
        'ffn2_w_down': dense((DEPTH, D_FF, D_MODEL), D_FF),
        'mix_norm': gain((DEPTH, D_MODEL)),
        'rec_w_in': dense((nA, D_MODEL, 2 * D_RNN), D_MODEL),
        'rec_conv_w': dense((nA, CONV_WIDTH, D_RNN), CONV_WIDTH),
        'rec_conv_b': bias((nA, D_RNN)),
        'rec_w_a': dense((nA, N_LRU_BLOCKS, LRU_BLOCK, LRU_BLOCK), LRU_BLOCK),
        'rec_b_a': bias((nA, D_RNN)),
        'rec_w_x': dense((nA, N_LRU_BLOCKS, LRU_BLOCK, LRU_BLOCK), LRU_BLOCK),
        'rec_b_x': bias((nA, D_RNN)),
        'rec_lambda': rec_lambda,
        'rec_w_out': dense((nA, D_RNN, D_MODEL), D_RNN),
        'kv_norm': gain((D_MODEL,)),
        'w_k': dense((D_MODEL, 2 * N_HEADS * HEAD_DIM), D_MODEL),
        'w_v': dense((D_MODEL, 2 * N_HEADS * HEAD_DIM), D_MODEL),
        'k_norm': gain((HEAD_DIM,)),
        'lambda_k1': 0.1 * jax.random.normal(next(ks), (HEAD_DIM,), f32),
        'lambda_k2': 0.1 * jax.random.normal(next(ks), (HEAD_DIM,), f32),
        'attn_w_q': dense((nB, D_MODEL, 2 * N_HEADS * HEAD_DIM), D_MODEL),
        'q_norm': gain((nB, HEAD_DIM)),
        'lambda_q1': 0.1 * jax.random.normal(next(ks), (nB, HEAD_DIM), f32),
        'lambda_q2': 0.1 * jax.random.normal(next(ks), (nB, HEAD_DIM), f32),
        'sub_norm': gain((nB, 2 * HEAD_DIM)),
        'attn_w_o': dense((nB, 2 * N_HEADS * HEAD_DIM, D_MODEL), 2 * N_HEADS * HEAD_DIM),
    }

def second_block(x, ffn1_norm, ffn1_w_gate, ffn1_w_up, ffn1_w_down,
              ffn2_norm, ffn2_w_gate, ffn2_w_up, ffn2_w_down, mix_norm,
              rec_w_in, rec_conv_w, rec_conv_b, rec_w_a, rec_b_a, rec_w_x, rec_b_x,
              rec_lambda, rec_w_out, kv_norm, w_k, w_v, k_norm, lambda_k1, lambda_k2,
              attn_w_q, q_norm, lambda_q1, lambda_q2, sub_norm, attn_w_o):
    S = x.shape[1]
    cos, sin = rope_tables(S)
    k_shared, v_shared = None, None
    for layer in range(DEPTH):
        if layer == N_A_LAYERS:
            k_shared, v_shared = shared_kv(x, kv_norm, w_k, w_v, k_norm, cos, sin)
        x = x + 0.5 * swiglu(rmsnorm_2(x, ffn1_norm[layer]), ffn1_w_gate[layer],
                             ffn1_w_up[layer], ffn1_w_down[layer])
        h = rmsnorm_2(x, mix_norm[layer])
        if layer < N_A_LAYERS:
            a = layer
            x = x + recurrent_block(h, rec_w_in[a], rec_conv_w[a], rec_conv_b[a], rec_w_a[a],
                                    rec_b_a[a], rec_w_x[a], rec_b_x[a], rec_lambda[a], rec_w_out[a])
        else:
            j = layer - N_A_LAYERS
            lambda_init = 0.8 - 0.6 * math.exp(-0.3 * layer)
            x = x + diff_attention(h, k_shared, v_shared, attn_w_q[j], q_norm[j], lambda_q1[j],
                                   lambda_q2[j], lambda_k1, lambda_k2, sub_norm[j], attn_w_o[j],
                                   cos, sin, lambda_init)
        x = x + 0.5 * swiglu(rmsnorm_2(x, ffn2_norm[layer]), ffn2_w_gate[layer],
                             ffn2_w_up[layer], ffn2_w_down[layer])
    return x


def setup_inputs(seed=0):
    out = dict(first_inputs(seed))
    for name, value in second_inputs(seed + 1).items():
        if name != "x":
            out[name + "_2"] = value
    return out


def reference(
    x, c, ctx, c_ctx, ada_w, ada_b, norm1_g, norm2_g, ffn_w_up, ffn_conv_w, ffn_conv_b,
    ffn_w_down, att_w_in, mla_qa_g, mla_w_qb, mla_kva_g, mla_w_kvb, mla_q_g, mla_k_g, gqa_q_g,
    gqa_k_g, att_w_out, ml_w_in, ml_conv_w, ml_conv_b, ml_gate_b, ml_out_g, ml_w_out,
    ffn1_norm_2, ffn1_w_gate_2, ffn1_w_up_2, ffn1_w_down_2, ffn2_norm_2, ffn2_w_gate_2,
    ffn2_w_up_2, ffn2_w_down_2, mix_norm_2, rec_w_in_2, rec_conv_w_2, rec_conv_b_2, rec_w_a_2,
    rec_b_a_2, rec_w_x_2, rec_b_x_2, rec_lambda_2, rec_w_out_2, kv_norm_2, w_k_2, w_v_2,
    k_norm_2, lambda_k1_2, lambda_k2_2, attn_w_q_2, q_norm_2, lambda_q1_2, lambda_q2_2,
    sub_norm_2, attn_w_o_2,
):
    x = first_block(
        x, c, ctx, c_ctx, ada_w, ada_b, norm1_g, norm2_g, ffn_w_up, ffn_conv_w, ffn_conv_b,
        ffn_w_down, att_w_in, mla_qa_g, mla_w_qb, mla_kva_g, mla_w_kvb, mla_q_g, mla_k_g,
        gqa_q_g, gqa_k_g, att_w_out, ml_w_in, ml_conv_w, ml_conv_b, ml_gate_b, ml_out_g,
        ml_w_out,
    )
    return second_block(
        x, ffn1_norm_2, ffn1_w_gate_2, ffn1_w_up_2, ffn1_w_down_2, ffn2_norm_2, ffn2_w_gate_2,
        ffn2_w_up_2, ffn2_w_down_2, mix_norm_2, rec_w_in_2, rec_conv_w_2, rec_conv_b_2,
        rec_w_a_2, rec_b_a_2, rec_w_x_2, rec_b_x_2, rec_lambda_2, rec_w_out_2, kv_norm_2, w_k_2,
        w_v_2, k_norm_2, lambda_k1_2, lambda_k2_2, attn_w_q_2, q_norm_2, lambda_q1_2,
        lambda_q2_2, sub_norm_2, attn_w_o_2,
    )


_drawn_inputs = setup_inputs


def setup_inputs(seed=0):
    import zlib

    import numpy as np

    out = dict(_drawn_inputs(seed))
    spreads = {}
    factors = {'norm1_g': 3.262,
     'ffn_conv_b': 7.068,
     'mla_qa_g': 8.0,
     'mla_kva_g': 7.062,
     'mla_q_g': 8.0,
     'mla_k_g': 8.0,
     'gqa_q_g': 8.0,
     'gqa_k_g': 8.0,
     'ml_conv_b': 7.579,
     'ml_out_g': 2.991,
     'ffn1_norm_2': 4.966,
     'ffn2_norm_2': 5.804,
     'mix_norm_2': 3.497,
     'rec_b_a_2': 8.0,
     'rec_b_x_2': 8.0,
     'kv_norm_2': 4.44,
     'k_norm_2': 8.0,
     'q_norm_2': 8.0,
     'lambda_q1_2': 6.787,
     'lambda_q2_2': 12.041,
     'sub_norm_2': 131.707}
    for name, (base, spread) in spreads.items():
        noise = np.random.default_rng([zlib.crc32(name.encode()), seed]).standard_normal(out[name].shape)
        drawn = base * np.exp(spread * noise) if base else spread * noise
        out[name] = __import__('jax').numpy.asarray(drawn.astype(out[name].dtype))
    for name, factor in factors.items():
        out[name] = (out[name] * factor).astype(out[name].dtype)
    return out
```

```python
from contextlib import ExitStack

import numpy as np
import concourse.bass as bass
from concourse import mybir

F32 = mybir.dt.float32
ALU = mybir.AluOpType
ACT = mybir.ActivationFunctionType
AX = mybir.AxisListType

P = 128
D = 1024
KT = 8
NL = 512
NC = 256
NT = NC + NL
FT = 22
EPS = 1e-6
SUB_EPS = 1e-5
LAMBDA_INIT = 0.8 - 0.6 * float(np.exp(-0.3))
RING = 4
SLOT = 2048
ARENA = 28300


def vec_columns():
    at, n = {}, 0
    for name, k in [
        ("c", 8), ("c_ctx", 8), ("ada_b", 96), ("norm1_g", 16), ("norm2_g", 16),
        ("ffn_conv_w", 132), ("ffn_conv_b", 44), ("mla_qa_g", 3), ("mla_kva_g", 2),
        ("mla_q_g", 1), ("mla_k_g", 1), ("gqa_q_g", 1), ("gqa_k_g", 1),
        ("ml_conv_w", 24), ("ml_conv_b", 8), ("ml_gate_b", 1), ("ml_out_g", 8),
        ("ffn1_norm_2", 16), ("ffn2_norm_2", 16), ("mix_norm_2", 16), ("rec_conv_w_2", 32),
        ("rec_conv_b_2", 8), ("rec_b_a_2", 8), ("rec_b_x_2", 8), ("rec_lambda_2", 8),
        ("kv_norm_2", 8), ("k_norm_2", 1), ("q_norm_2", 1), ("sub_norm_2", 1),
        ("lambda_q1_2", 1), ("lambda_q2_2", 1), ("lambda_k1_2", 1), ("lambda_k2_2", 1),
    ]:
        at[name] = (n, k)
        n += k
    return at, n


VEC_AT, NVEC = vec_columns()


def weight_chunks():
    down = [8 * 256, 8 * 256, 6 * 256] * 4
    return {
        "ada0": [2048] * 24, "ada1": [2048] * 24,
        "up0": [2048] * 22, "down0": down, "up1": [2048] * 22, "down1": down,
        "att_cq": [1024] * 3, "att_ckv": [1024] * 2, "att_kr": [256], "att_gq": [1024] * 4,
        "att_gk": [1024], "att_gv": [1024],
        "qb": [3 * 96 * 4] * 2, "kb": [2 * 64 * 8], "vb": [2 * 512], "att_out": [2048] * 4,
        "ml_qk": [1024] * 8, "ml_v": [2048] * 4, "ml_o": [1024] * 8, "ml_g": [1024],
        "ml_out": [2048] * 4,
        "s_up10": [2048] * 22, "s_down10": down, "s_up20": [2048] * 22, "s_down20": down,
        "s_up11": [2048] * 22, "s_down11": down, "s_up21": [2048] * 22, "s_down21": down,
        "rec_in": [2048] * 8, "rec_g": [2048], "rec_out": [2048] * 4,
        "wk": [2048] * 4, "wv": [2048] * 4, "wq": [2048] * 4, "wo": [2048] * 4,
    }


CHUNKS = weight_chunks()

CONSTS = [("ident", 128), ("ones", 128), ("bones", 128), ("rot_g", 128), ("rot_m", 128), ("rot_2", 128),
          ("mask_f", 128), ("mask_b", 128), ("sel", 1024), ("rope_m", 1024), ("rope_g", 1024), ("rope_2", 1024)]


def const_columns():
    at, n = {}, 0
    for name, k in CONSTS:
        at[name] = (n, k)
        n += k
    return at, n


CONST_AT, NCONST = const_columns()


class Engine:

    def __init__(self, e, sem, serial=False):
        self.e, self.sem, self.n, self.seen, self.serial = e, sem, 0, {}, serial

    def wait(self, *tokens):
        for t in tokens:
            if t is None:
                continue
            if isinstance(t, list):
                self.wait(*t)
                continue
            sem, value, key = t
            if self.seen.get(key, 0) < value:
                self.seen[key] = value
                self.e.wait_ge(sem, value)

    def done(self, ins):
        self.n += 1
        ins.then_inc(self.sem, 1)
        token = (self.sem, self.n, id(self))
        if self.serial:
            self.wait(token)
        return token


class Slot:

    def __init__(self, ap):
        self.ap, self.free = ap, []


class Rotor:
    def __init__(self, slots):
        self.slots, self.i = slots, 0

    def take(self):
        s = self.slots[self.i % len(self.slots)]
        self.i += 1
        return s


def build(nc, xT, ctxT, vecs, consts, weights, outT, stop=99):
    with ExitStack() as ctx:
        def sb(name, shape):
            return ctx.enter_context(nc.sbuf_tensor(name, shape, F32))

        def sem(name):
            return ctx.enter_context(nc.semaphore(name))

        PE = Engine(nc.tensor, sem("s_pe"))
        VE = Engine(nc.vector, sem("s_ve"))
        SC = Engine(nc.scalar, sem("s_sc"))
        GP = Engine(nc.gpsimd, sem("s_gp"), serial=True)
        pe, ve, sc, gp = PE.e, VE.e, SC.e, GP.e

        X = sb("X", [P, KT, NL])
        XC = sb("XC", [P, KT, NC])
        H = sb("H", [P, KT, NL])
        HC = sb("HC", [P, KT, NC])
        VEC = sb("VEC", [P, NVEC])
        MOD = sb("MOD", [P, 2, 48, 2])
        GS = sb("GS", [P, 2, 2, 8, 2])
        CS = sb("CS", [P, 8, 2])
        RS = sb("RS", [P, NT])
        MN = sb("MN", [P, 64])
        CONST = sb("CONST", [P, 384])
        SM = sb("SM", [P, 128])
        TMP = sb("TMP", [P, 4, NL])
        ringt = sb("ring", [P, RING, SLOT])
        A = sb("A", [P, ARENA])
        ps = ctx.enter_context(nc.psum_tensor("ps", [P, 8, 512], F32))

        banks = [Slot(ps[:, i, :]) for i in range(8)]
        brot = [0]

        def bank(n=1):
            while brot[0] % n:
                brot[0] += 1
            i = brot[0] % 8
            brot[0] += n
            return banks[i] if n == 1 else banks[i:i + n]

        tmp = Rotor([Slot(TMP[:, i, :]) for i in range(4)])
        ring = [Slot(ringt[:, i, :]) for i in range(RING)]
        ring_sem = [sem(f"s_w{i}") for i in range(RING)]
        ring_n = [0]
        offsets = {}
        for name, sizes in CHUNKS.items():
            o = [0]
            for f in sizes:
                o.append(o[-1] + f * P)
            offsets[name] = o

        def load(name, i):
            k = ring_n[0] % RING
            turn = ring_n[0] // RING + 1
            ring_n[0] += 1
            s = ring[k]
            for t in s.free:
                sp_wait(t)
            f = CHUNKS[name][i]
            o = offsets[name]
            nc.sync.dma_start(s.ap[:, 0:f], weights[name][o[i]:o[i + 1]].rearrange("(p f) -> p f", p=P))\
                .then_inc(ring_sem[k], 16)
            return s, (ring_sem[k], 16 * turn, f"w{k}")

        sp_seen = {}

        def sp_wait(t):
            s, value, key = t
            if sp_seen.get(key, 0) < value:
                sp_seen[key] = value
                nc.sync.wait_ge(s, value)

        nload = [0]

        def fetch(dst, src, *tokens):
            s = sem(f"s_l{nload[0]}")
            nload[0] += 1
            SC.wait(*tokens)
            sc.dma_start(dst, src).then_inc(s, 16)
            return (s, 16, f"l{nload[0]}")

        def vec(name, i=0):
            o, _ = VEC_AT[name]
            return VEC[:, o + i:o + i + 1]

        def const(name):
            o, n = CONST_AT[name]
            return consts[:, o:o + n]

        ident = CONST[:, 0:128]
        ones = CONST[:, 128:256]
        bones = CONST[:, 256:384]
        t_const = fetch(CONST[:, :], consts[:, 0:384])
        t_vec = fetch(VEC[:, :], vecs)
        t_x = fetch(X[:, :, :], xT.rearrange("(k p) t -> p k t", p=P))
        t_xc = fetch(XC[:, :, :], ctxT.rearrange("(k p) t -> p k t", p=P))
        for e in (PE, VE, SC, GP):
            e.wait(t_const, t_vec)

        state = {"x": [t_x] * KT, "xc": [t_xc] * KT, "h_free": [], "hc_free": [], "arena_free": []}

        def mm_group(out, pairs, deps):
            PE.wait(*deps)
            n = len(pairs)
            for i, (l, r) in enumerate(pairs):
                ins = pe.matmul(out, l, r, start=(i == 0), stop=(i == n - 1))
            return PE.done(ins)

        t_cs = SC.done(sc.activation(CS[:, :, 0], VEC[:, 0:8], ACT.Silu))
        t_cs = SC.done(sc.activation(CS[:, :, 1], VEC[:, 8:16], ACT.Silu))
        t_mod = {}

        def ada_chunk(layer, i):
            s, tl = load(f"ada{layer}", i)
            b = bank()
            w = s.ap.rearrange("p (k n) -> p k n", k=8)
            PE.wait(tl, t_cs, b.free)
            for j in range(2):
                for k in range(8):
                    ins = pe.matmul(b.ap[:, 2 * j:2 * j + 2], w[:, k, j * 128:(j + 1) * 128], CS[:, k, :],
                                    start=(k == 0), stop=(k == 7))
            tm = PE.done(ins)
            s.free = [tm]
            VE.wait(tm)
            o = VEC_AT["ada_b"][0] + 48 * layer + 2 * i
            for j in range(2):
                t = VE.done(ve.tensor_scalar(MOD[:, layer, 2 * i + j, :], b.ap[:, 2 * j:2 * j + 2],
                                             VEC[:, o + j:o + j + 1], None, ALU.add))
            b.free = [t]
            part = i // 4
            t_mod[(layer, part)] = t
            if i % 4 == 3 and part in (1, 4):
                which = 0 if part == 1 else 1
                g = VEC_AT[("norm1_g", "norm2_g")[which]][0] + 8 * layer
                VE.wait(t)
                for c in range(2):
                    t = VE.done(ve.scalar_tensor_tensor(
                        out=GS[:, layer, which, :, c], in0=MOD[:, layer, 8 * part:8 * part + 8, c], scalar=1.0,
                        in1=VEC[:, g:g + 8], op0=ALU.add, op1=ALU.mult))
                t_mod[(layer, part)] = t

        def mod(layer, part, m, c):
            return MOD[:, layer, part * 8 + m, c:c + 1]

        side = []

        def run_side(n=1):
            for _ in range(n):
                if side:
                    side.pop(0)()

        def rstd_of(b, rows, n, count, eps, out, tb, deps=()):
            s = tmp.take()
            SC.wait(tb, s.free)
            t = SC.done(sc.activation(s.ap[rows, 0:n], b.ap[rows, 0:n], ACT.Sqrt, bias=eps_ap(eps)[rows, :],
                                      scale=1.0 / count))
            b.free = [t]
            VE.wait(t, *deps)
            t = VE.done(ve.reciprocal(out, s.ap[rows, 0:n]))
            s.free = [t]
            return t

        t_eps = [VE.done(ve.memset(SM[:, 0:1], EPS)), VE.done(ve.memset(SM[:, 1:2], SUB_EPS))]
        SC.wait(t_eps)

        def eps_ap(eps):
            return SM[:, 0:1] if eps == EPS else SM[:, 1:2]

        rs_free = {}

        def norm(src, dst, n, tok, nk, count, gain, shift, dst_free, rs_off, deps=(), eps=EPS):
            b = bank()
            tb = None
            for k in range(nk):
                s = tmp.take()
                SC.wait(tok[k], s.free)
                ts = SC.done(sc.activation(s.ap[:, 0:n], src[:, k, :], ACT.Square))
                PE.wait(ts, b.free)
                tb = PE.done(pe.matmul(b.ap[:, 0:n], ones, s.ap[:, 0:n], start=(k == 0), stop=(k == nk - 1)))
                s.free = [tb]
            rs = RS[:, rs_off:rs_off + n]
            tr = rstd_of(b, slice(0, P), n, count, eps, rs, tb, [rs_free.get(rs_off)])
            out = []
            VE.wait(tr, *deps)
            VE.wait(dst_free)
            for k in range(nk):
                VE.wait(tok[k])
                t = VE.done(ve.scalar_tensor_tensor(out=dst[:, k, :], in0=src[:, k, :], scalar=gain(k), in1=rs,
                                                    op0=ALU.mult, op1=ALU.mult))
                rs_free[rs_off] = t
                if shift is not None:
                    SC.wait(t, *deps)
                    t = SC.done(sc.activation(dst[:, k, :], dst[:, k, :], ACT.Identity, bias=shift(k)))
                out.append(t)
            return out

        def norm_main(gain_of, shift_of, with_ctx, deps):
            r = [norm(X, H, NL, state["x"], 8, D, gain_of(0), shift_of and shift_of(0), state["h_free"], 0, deps)]
            if with_ctx:
                r.append(norm(XC, HC, NC, state["xc"], 8, D, gain_of(1), shift_of and shift_of(1),
                              state["hc_free"], NL, deps))
            return r

        def segments(with_ctx, h, hc, th):
            return [(h, NL, th[0])] + ([(hc, NC, th[1])] if with_ctx else [])

        def residual(m, seg, b, tb, scale):
            x, key = ((X, "x"), (XC, "xc"))[seg]
            VE.wait(tb, state[key][m])
            t = VE.done(ve.scalar_tensor_tensor(out=x[:, m, :], in0=b.ap[:, 0:x.shape[2]], scalar=scale,
                                                in1=x[:, m, :], op0=ALU.mult, op1=ALU.add))
            b.free = [t]
            state[key][m] = t

        def ffn(up, down, th, with_ctx, conv, scale, scale_dep):
            hid = A[:, 0:FT * NL].rearrange("p (f t) -> p f t", f=FT)
            hidc = A[:, FT * NL:FT * NT].rearrange("p (f t) -> p f t", f=FT)
            segs = segments(with_ctx, H, HC, th)
            t_hid = [[None] * FT for _ in segs]
            first = state["arena_free"]
            last = None
            for j in range(FT):
                run_side()
                s, tl = load(up, j)
                w = s.ap.rearrange("p (g k n) -> p g k n", g=2, k=8)
                for si, (h, n, tk) in enumerate(segs):
                    bg, bv = bank(), bank()
                    tg = mm_group(bg.ap[:, 0:n], [(w[:, 0, k, :], h[:, k, :]) for k in range(8)], [tl, tk, bg.free])
                    tv = mm_group(bv.ap[:, 0:n], [(w[:, 1, k, :], h[:, k, :]) for k in range(8)], [bv.free])
                    last = tv
                    s.free = [tv]
                    dst = (hid, hidc)[si][:, j, :]
                    a = tmp.take()
                    av, gv = a.ap[:, 0:n], bg.ap[:, 0:n]
                    if conv is None:
                        SC.wait(tg, a.free)
                        t = SC.done(sc.activation(av, gv, ACT.Silu))
                        bg.free = [t]
                    else:
                        o = VEC_AT["ffn_conv_w"][0] + 66 * conv + j
                        ob = VEC_AT["ffn_conv_b"][0] + 22 * conv + j
                        SC.wait(tg, a.free)
                        t = SC.done(sc.activation(av, gv, ACT.Identity, bias=VEC[:, ob:ob + 1],
                                                  scale=VEC[:, o + 22:o + 23]))
                        VE.wait(t)
                        t = VE.done(ve.scalar_tensor_tensor(out=av[:, 1:n], in0=gv[:, 0:n - 1], scalar=VEC[:, o:o + 1],
                                                            in1=av[:, 1:n], op0=ALU.mult, op1=ALU.add))
                        VE.wait(t)
                        t = VE.done(ve.scalar_tensor_tensor(out=av[:, 0:n - 1], in0=gv[:, 1:n],
                                                            scalar=VEC[:, o + 44:o + 45],
                                                            in1=av[:, 0:n - 1], op0=ALU.mult, op1=ALU.add))
                        bg.free = [t]
                        SC.wait(t)
                        t = SC.done(sc.activation(av, av, ACT.Silu))
                    VE.wait(t, tv, first)
                    t = VE.done(ve.tensor_tensor(dst, bv.ap[:, 0:n], av, ALU.mult))
                    a.free = [t]
                    bv.free = [t]
                    t_hid[si][j] = t
            state["h_free"] = [last]
            state["hc_free"] = [last]
            for mp in range(4):
                acc = [[bank() for _ in range(2)] for _ in segs]
                for kg in range(3):
                    run_side()
                    s, tl = load(down, 3 * mp + kg)
                    ks = range(8 * kg, min(8 * kg + 8, FT))
                    w = s.ap[:, 0:len(ks) * 256].rearrange("p (k n) -> p k n", k=len(ks))
                    for si, (_, n, _) in enumerate(segs):
                        h = (hid, hidc)[si]
                        for j in range(2):
                            b = acc[si][j]
                            PE.wait(tl, b.free)
                            for k in ks:
                                PE.wait(t_hid[si][k])
                                ins = pe.matmul(b.ap[:, 0:n], w[:, k - 8 * kg, j * 128:(j + 1) * 128], h[:, k, :],
                                                start=(k == 0), stop=(k == FT - 1))
                            t = PE.done(ins)
                            if kg == 2:
                                VE.wait(scale_dep)
                                residual(2 * mp + j, si, b, t, scale(2 * mp + j, si))
                    s.free = [t]
            state["arena_free"] = [t]

        def project_out(name, rhs, segs, tok, scale, scale_dep):
            for c in range(4):
                s, tl = load(name, c)
                w = s.ap.rearrange("p (k n) -> p k n", k=8)
                for si, n in segs:
                    for j in range(2):
                        b = bank()
                        t = mm_group(b.ap[:, 0:n], [(w[:, k, j * 128:(j + 1) * 128], rhs(si, k)) for k in range(8)],
                                     [tl, b.free, tok])
                        VE.wait(scale_dep)
                        residual(2 * c + j, si, b, t, scale(2 * c + j, si))
                s.free = [t]
            return t

        def attention(jobs, p_slots):
            prot = Rotor(p_slots)
            mnr = Rotor([Slot(MN[:, 4 * i:4 * i + 4]) for i in range(4)])

            def maxima(j):
                d, nq = j["d"], j["nq"]
                m = mnr.take()
                j["m"] = m
                toks = []
                for qb in range(nq // 128):
                    nk = 128 * (qb + 1) if j["causal"] else j["nk"]
                    q = j["q"][0:d, qb * 128:(qb + 1) * 128]
                    if nk <= 512:
                        b = bank()
                        t = mm_group(b.ap[:, 0:nk], [(q, j["k"][0:d, 0:nk])], [j["deps"], b.free])
                        VE.wait(t, m.free)
                        if j["causal"]:
                            t = VE.done(ve.tensor_reduce(m.ap[0:64, qb:qb + 1], b.ap[0:64, 0:nk - 64], AX.X, ALU.max))
                            t = VE.done(ve.tensor_reduce(m.ap[64:128, qb:qb + 1], b.ap[64:128, 0:nk], AX.X, ALU.max))
                        else:
                            t = VE.done(ve.tensor_reduce(m.ap[:, qb:qb + 1], b.ap[:, 0:nk], AX.X, ALU.max))
                        b.free = [t]
                    else:
                        b0, b1 = bank(2)
                        i0 = banks.index(b0)
                        half = nk // 2
                        PE.wait(j["deps"], b0.free, b1.free)
                        pe.matmul(b0.ap[:, 0:half], q, j["k"][0:d, 0:half], start=True, stop=True)
                        t = PE.done(pe.matmul(b1.ap[:, 0:half], q, j["k"][0:d, half:nk], start=True, stop=True))
                        VE.wait(t, m.free)
                        t = VE.done(ve.tensor_reduce(m.ap[:, qb:qb + 1], ps[:, i0:i0 + 2, 0:half], AX.XY, ALU.max))
                        b0.free = [t]
                        b1.free = [t]
                j["t_max"] = t

            def row(j):
                d, nq = j["d"], j["nq"]
                b = bank()
                PE.wait(j["t_max"], b.free)
                for qb in range(nq // 128):
                    ins = pe.matmul(b.ap[d:d + 1, qb * 128:(qb + 1) * 128], j["m"].ap[:, qb:qb + 1], ident,
                                    start=True, stop=True)
                t = PE.done(ins)
                j["m"].free = [t]
                SC.wait(t)
                t = SC.done(sc.activation(j["q"][d:d + 1, 0:nq], b.ap[d:d + 1, 0:nq], ACT.Copy, scale=-1.0))
                b.free = [t]
                j["t_row"] = t

            def probs(j):
                d, nq = j["d"], j["nq"]
                j["p"] = []
                for kb in range(j["nk"] // 128):
                    q0 = 128 * kb if j["causal"] else 0
                    b = bank()
                    t = mm_group(b.ap[:, 0:nq - q0], [(j["k"][0:d + 1, kb * 128:(kb + 1) * 128], j["q"][0:d + 1, q0:nq])],
                                 [j["t_row"], j["t_one"], b.free])
                    s = prot.take()
                    SC.wait(t, s.free)
                    if j["causal"]:
                        GP.wait(s.free)
                        tz = GP.done(gp.memset(s.ap[64:128, 0:64], 0.0))
                        sc.activation(s.ap[0:64, 0:nq - q0], b.ap[0:64, 0:nq - q0], ACT.Exp, scale=j["scale"])
                        t = SC.done(sc.activation(s.ap[64:128, 64:nq - q0], b.ap[64:128, 64:nq - q0], ACT.Exp,
                                                  scale=j["scale"]))
                        b.free = [t]
                        t = [t, tz]
                    else:
                        t = SC.done(sc.activation(s.ap[:, 0:nq], b.ap[:, 0:nq], ACT.Exp, scale=j["scale"]))
                        b.free = [t]
                    j["p"].append((s, q0, t))

            def values(j):
                nq = j["nq"]
                n = len(j["p"])
                outs = []
                for v in j["v"]:
                    b = bank()
                    PE.wait(b.free, j["t_v"])
                    for i, (s, q0, t) in enumerate(j["p"]):
                        PE.wait(t)
                        ins = pe.matmul(b.ap[:, q0:nq], v(i), s.ap[:, 0:nq - q0], start=(i == 0), stop=(i == n - 1),
                                        skip_group_check=j["causal"])
                    t = PE.done(ins)
                    outs.append((b, t))
                for s, _, _ in j["p"]:
                    s.free = [t]
                j["finish"](outs)

            n = len(jobs)
            for i in range(n + 2):
                if i < n:
                    maxima(jobs[i])
                if 0 <= i - 1 < n:
                    row(jobs[i - 1])
                if 0 <= i - 2 < n:
                    values(jobs[i - 2])
                if 0 <= i - 1 < n:
                    probs(jobs[i - 1])

        def even_mixer():
            o = [0]

            def area(n):
                o[0] += n
                assert o[0] <= ARENA, o[0]
                return A[:, o[0] - n:o[0]]

            QL = area(8 * NL).rearrange("p (h t) -> p h t", h=8)
            QC = area(8 * NC).rearrange("p (h t) -> p h t", h=8)
            K = area(8 * NT).rearrange("p (h t) -> p h t", h=8)
            V = area(6 * 4 * 192).rearrange("p (b h n) -> p b h n", b=6, h=4)
            VG = area(6 * 192).rearrange("p (b n) -> p b n", b=6)
            GR = area(5 * NT).rearrange("p (h t) -> p h t", h=5)
            CP = area(5 * NT)
            C = CP.rearrange("p (h t) -> p h t", h=5)
            RM = area(1024)
            RG = area(1024)
            ROT = area(256)
            free = state["arena_free"]
            t_rm = fetch(RM, const("rope_m"), free)
            t_rg = fetch(RG, const("rope_g"), free)
            ro = CONST_AT["rot_g"][0]
            t_ro = fetch(ROT, consts[:, ro:ro + 256], free)
            rot_g = ROT[:, 0:128]
            rot_m = ROT[:, 128:256]

            layer = 0
            gain = lambda c: (lambda k: GS[:, layer, 0, k, c:c + 1])
            shift = lambda c: (lambda k: mod(layer, 0, k, c))
            th = norm_main(gain, shift, True, [t_mod[(0, 0)], t_mod[(0, 1)]])
            segs = [(H, NL, th[0], NC), (HC, NC, th[1], 0)]

            def plain(name, i, dst, m=128, base=0, copy=None):
                run_side()
                s, tl = load(name, i)
                w = s.ap[:, 0:8 * m].rearrange("p (k n) -> p k n", k=8)
                ts = []
                for h, n, tk, off in segs:
                    b = bank()
                    t = mm_group(b.ap[base:base + m, 0:n], [(w[:, k, :], h[:, k, :]) for k in range(8)],
                                 [tl, tk, b.free])
                    last = t
                    if copy is not None:
                        copy(b, n, off, t)
                        continue
                    SC.wait(t)
                    t = SC.done(sc.activation(dst[:, off:off + n], b.ap[:, 0:n], ACT.Copy))
                    b.free = [t]
                    ts.append(t)
                s.free = [last]
                return ts

            SC.wait(free)
            GP.wait(free)
            VE.wait(free)
            t_c = [plain("att_cq", i, C[:, i, :]) for i in range(3)]
            t_c += [plain("att_ckv", i, C[:, 3 + i, :]) for i in range(2)]
            t_kr = []

            def kr_copy(b, n, off, t):
                SC.wait(t)
                for h in range(8):
                    t = SC.done(sc.activation(K[64:96, h, off:off + n], b.ap[64:96, 0:n], ACT.Copy))
                b.free = [t]
                t_kr.append(t)

            plain("att_kr", 0, None, 32, 64, kr_copy)
            t_g = [plain("att_gq", i, GR[:, i, :]) for i in range(4)]
            t_g.append(plain("att_gk", 0, GR[:, 4, :]))
            run_side()
            s, tl = load("att_gv", 0)
            w = s.ap[:, 0:1024].rearrange("p (k n) -> p k n", k=8)
            tv1 = GP.done(gp.memset(VG[:, :, 64:128], 1.0))
            t_vg = [tv1]

            def h_block(tb, k):
                return HC[:, k, tb * 128:(tb + 1) * 128] if tb < 2 else H[:, k, (tb - 2) * 128:(tb - 1) * 128]

            for tb in range(6):
                b = bank()
                t = mm_group(b.ap[:, 0:128], [(h_block(tb, k), w[:, k, :]) for k in range(8)], [tl, b.free])
                t_hlast = t
                VE.wait(t)
                t = VE.done(ve.tensor_copy(VG[:, tb, :].rearrange("p (a n) -> p a n", a=3)[:, 0:3:2, :],
                                           b.ap[:, 0:128].rearrange("p (a n) -> p a n", a=2)))
                b.free = [t]
            t_vg.append(t)
            s.free = [t_hlast]
            run_side(99)

            t_cn = [[None] * 2 for _ in range(5)]
            for lo, hi, name in ((0, 3, "mla_qa_g"), (3, 5, "mla_kva_g")):
                for si, (off, n) in enumerate(((NC, NL), (0, NC))):
                    v = C[:, lo:hi, off:off + n]
                    r = norm(v, v, n, [t_c[k][si] for k in range(lo, hi)], hi - lo, 128 * (hi - lo),
                             lambda k: vec(name, k), None, [], NL * si)
                    for k in range(lo, hi):
                        t_cn[k][si] = r[k - lo]

            def mla_head(b, tb, src_rows, n, dst, g, dst_free, rope_tok):
                s = tmp.take()
                src = b.ap[0:96, 0:n] if b is not None else dst
                SC.wait(tb, s.free)
                t = SC.done(sc.activation(s.ap[0:96, 0:n], src, ACT.Square))
                b2 = bank()
                tq = mm_group(b2.ap[0:96, 0:n], [(ones[0:96, 0:96], s.ap[0:96, 0:n])], [t, b2.free])
                s.free = [tq]
                r = tmp.take()
                VE.wait(r.free)
                t = rstd_of(b2, slice(0, 96), n, 96, EPS, r.ap[0:96, 0:n], tq)
                VE.wait(t, tb, dst_free)
                t = VE.done(ve.scalar_tensor_tensor(out=dst, in0=src, scalar=VEC[0:96, g:g + 1], in1=r.ap[0:96, 0:n],
                                                    op0=ALU.mult, op1=ALU.mult))
                r.free = [t]
                if b is not None:
                    b.free = [t]
                if rope_tok is None:
                    return t
                b3 = bank()
                tr = mm_group(b3.ap[64:96, 0:n], [(rot_m[64:96, 64:96], dst[64:96, :])], [t, t_ro, b3.free])
                u = tmp.take()
                VE.wait(tr, u.free, rope_tok)
                t1 = VE.done(ve.tensor_tensor(u.ap[64:96, 0:n], b3.ap[64:96, 0:n], RM[64:96, 512:1024], ALU.mult))
                b3.free = [t1]
                t2 = VE.done(ve.tensor_tensor(dst[64:96, :], dst[64:96, :], RM[64:96, 0:512], ALU.mult))
                VE.wait(t1, t2)
                t = VE.done(ve.tensor_tensor(dst[64:96, :], dst[64:96, :], u.ap[64:96, 0:n], ALU.add))
                u.free = [t]
                return t

            tokspan = ((NC, NL), (0, NC))
            t_q = [[None] * 2 for _ in range(8)]
            t_k = [[None] * 2 for _ in range(8)]
            gq = VEC_AT["mla_q_g"][0]
            gk = VEC_AT["mla_k_g"][0]
            for half in range(2):
                s, tl = load("qb", half)
                w = s.ap[:, 0:1152].rearrange("p (h k n) -> p h k n", h=4, k=3)
                for h4 in range(4):
                    h = 4 * half + h4
                    for si, (off, n) in enumerate(tokspan):
                        b = bank()
                        tb = mm_group(b.ap[0:96, 0:n], [(w[:, h4, k, :], C[:, k, off:off + n]) for k in range(3)],
                                      [tl, b.free, [t_cn[k][si] for k in range(3)]])
                        s.free = [tb]
                        dst = (QL, QC)[si][0:96, h, :]
                        t_q[h][si] = mla_head(b, tb, None, n, dst, gq, [], t_rm if si == 0 else None)
            s, tl = load("kb", 0)
            w = s.ap[:, 0:1024].rearrange("p (h k n) -> p h k n", h=8, k=2)
            for h in range(8):
                for si, (off, n) in enumerate(tokspan):
                    b = bank()
                    tb = mm_group(b.ap[0:64, 0:n], [(w[:, h, k, :], C[:, 3 + k, off:off + n]) for k in range(2)],
                                  [tl, b.free, [t_cn[3 + k][si] for k in range(2)]])
                    s.free = [tb]
                    SC.wait(tb)
                    t = SC.done(sc.activation(K[0:64, h, off:off + n], b.ap[0:64, 0:n], ACT.Copy))
                    b.free = [t]
                    t_k[h][si] = mla_head(None, [t, t_kr], None, n, K[0:96, h, off:off + n], gk, [],
                                          t_rm if si == 0 else None)
            t_one = GP.done(gp.memset(K[96:97, :, :], 1.0))
            s, tl = load("vb", 0)
            w = s.ap[:, 0:1024].rearrange("p (k n) -> p k n", k=2)
            t_v = [GP.done(gp.memset(V[:, :, :, 64:128], 1.0))]
            for tb in range(6):
                b = bank()
                t = mm_group(b.ap[:, 0:512], [(C[:, 3 + k, tb * 128:(tb + 1) * 128], w[:, k, :]) for k in range(2)],
                             [tl, b.free])
                s.free = [t]
                t_clast = t
                VE.wait(t)
                t = VE.done(ve.tensor_copy(V[:, tb, :, 0:64],
                                           b.ap[:, 0:512].rearrange("p (h a n) -> p h a n", h=4, a=2)[:, :, 0, :]))
                t = VE.done(ve.tensor_copy(V[:, tb, :, 128:192],
                                           b.ap[:, 0:512].rearrange("p (h a n) -> p h a n", h=4, a=2)[:, :, 1, :]))
                b.free = [t]
            t_v.append(t)

            t_mix = []

            def finish_at(tile, odd, si, nq):
                def finish(outs):
                    (b, tb), = outs
                    o0, s0 = (64, 0) if odd else (0, 64)
                    r = tmp.take()
                    VE.wait(tb, r.free)
                    t = VE.done(ve.reciprocal(r.ap[o0:o0 + 64, 0:nq], b.ap[s0:s0 + 64, 0:nq]))
                    VE.wait(t, t_hlast)
                    dst = (H, HC)[si][o0:o0 + 64, tile, :]
                    t = VE.done(ve.tensor_tensor(dst, b.ap[o0:o0 + 64, 0:nq], r.ap[o0:o0 + 64, 0:nq], ALU.mult))
                    r.free = [t]
                    b.free = [t]
                    t_mix.append(t)
                return finish

            p_slots = [Slot(CP[:, 512 * i:512 * i + 512]) for i in range(7)]
            for p in p_slots:
                p.free = [t_clast]
            jobs = []
            for h in range(8):
                vo = 0 if h % 2 == 0 else 64
                for si, nq, nk in ((0, NL, NT), (1, NC, NC)):
                    jobs.append(dict(
                        d=96, scale=96.0 ** -0.5, q=(QL, QC)[si][:, h, :], k=K[:, h, 0:nk], nq=nq, nk=nk, causal=False,
                        deps=[t_q[h][si], t_k[h]], t_one=t_one, t_v=t_v,
                        v=[lambda kb, h=h, vo=vo: V[:, kb, h // 2, vo:vo + 128]],
                        finish=finish_at(h // 2, h % 2, si, nq)))
            attention(jobs, p_slots)
            t_after = (PE.sem, PE.n, id(PE))

            def pair(i, si, off, n, g, dst0, dst1):
                src = GR[:, i, off:off + n]
                s = tmp.take()
                SC.wait(t_g[i][si], s.free)
                t = SC.done(sc.activation(s.ap[:, 0:n], src, ACT.Square))
                b2 = bank()
                tq = mm_group(b2.ap[:, 0:n], [(bones, s.ap[:, 0:n])], [t, b2.free])
                s.free = [tq]
                r = tmp.take()
                VE.wait(r.free)
                t = rstd_of(b2, slice(0, P), n, 64, EPS, r.ap[:, 0:n], tq)
                VE.wait(t, t_after)
                if si == 1:
                    for half, dst in ((0, dst0), (64, dst1)):
                        t = VE.done(ve.scalar_tensor_tensor(
                            out=dst, in0=src[half:half + 64, :], scalar=VEC[half:half + 64, g:g + 1],
                            in1=r.ap[half:half + 64, 0:n], op0=ALU.mult, op1=ALU.mult))
                    r.free = [t]
                    return t
                t = VE.done(ve.scalar_tensor_tensor(out=src, in0=src, scalar=VEC[:, g:g + 1], in1=r.ap[:, 0:n],
                                                    op0=ALU.mult, op1=ALU.mult))
                r.free = [t]
                b3 = bank()
                tr = mm_group(b3.ap[:, 0:n], [(rot_g, src)], [t, b3.free])
                u = tmp.take()
                VE.wait(tr, u.free, t_rg)
                t1 = VE.done(ve.tensor_tensor(u.ap[:, 0:n], b3.ap[:, 0:n], RG[:, 512:1024], ALU.mult))
                b3.free = [t1]
                t2 = VE.done(ve.tensor_tensor(src, src, RG[:, 0:512], ALU.mult))
                VE.wait(t1, t2)
                for half, dst in ((0, dst0), (64, dst1)):
                    t = VE.done(ve.tensor_tensor(dst, src[half:half + 64, :], u.ap[half:half + 64, 0:n], ALU.add))
                u.free = [t]
                return t

            t_q = [[None] * 2 for _ in range(8)]
            t_k = [None] * 2
            GP.wait(t_after)
            t_one = GP.done(gp.memset(K[64:65, 0:2, :], 1.0))
            VE.wait(t_one)
            for si, (off, n) in enumerate(tokspan):
                t_k[si] = pair(4, si, off, n, VEC_AT["gqa_k_g"][0], K[0:64, 0, off:off + n], K[0:64, 1, off:off + n])
            for i in range(4):
                for si, (off, n) in enumerate(tokspan):
                    Q = (QL, QC)[si]
                    t = pair(i, si, off, n, VEC_AT["gqa_q_g"][0], Q[0:64, 2 * i, :], Q[0:64, 2 * i + 1, :])
                    t_q[2 * i][si] = t
                    t_q[2 * i + 1][si] = t
            jobs = []
            for h in range(8):
                g = h // 4
                for si, nq, nk in ((0, NL, NT), (1, NC, NC)):
                    def finish(outs, h=h, g=g, si=si, nq=nq):
                        (b, tb), = outs
                        o0, s0 = (64, 0) if g else (0, 64)
                        d0 = 64 * (h % 2)
                        r = tmp.take()
                        VE.wait(tb, r.free)
                        t = VE.done(ve.reciprocal(r.ap[o0:o0 + 64, 0:nq], b.ap[s0:s0 + 64, 0:nq]))
                        VE.wait(t)
                        dst = (H, HC)[si][d0:d0 + 64, 4 + h // 2, :]
                        t = VE.done(ve.tensor_tensor(dst, b.ap[o0:o0 + 64, 0:nq], r.ap[o0:o0 + 64, 0:nq], ALU.mult))
                        r.free = [t]
                        b.free = [t]
                        t_mix.append(t)

                    jobs.append(dict(
                        d=64, scale=0.125, q=(QL, QC)[si][:, h, :], k=K[:, g, 0:nk], nq=nq, nk=nk, causal=False,
                        deps=[t_q[h][si], t_k], t_one=t_one, t_v=t_vg,
                        v=[lambda kb, g=g: VG[:, kb, 64 * g:64 * g + 128]], finish=finish))
            attention(jobs, p_slots)
            t = project_out("att_out", lambda si, k: (H, HC)[si][:, k, :], [(0, NL), (1, NC)], t_mix,
                            lambda m, si: mod(0, 2, m, si), t_mod[(0, 2)])
            state["h_free"] = [t]
            state["hc_free"] = [t]
            state["arena_free"] = [t]

        def odd_mixer():
            o = [0]

            def area(n):
                o[0] += n
                assert o[0] <= ARENA, o[0]
                return A[:, o[0] - n:o[0]]

            KK = area(4 * NT).rearrange("p (h t) -> p h t", h=4)
            QQ = area(4 * NL).rearrange("p (h t) -> p h t", h=4)
            V = area(6 * 1024).rearrange("p (b n) -> p b n", b=6)
            O = area(8 * NL).rearrange("p (h t) -> p h t", h=8)
            PP = [Slot(area(NL)) for _ in range(6)]
            DD = [Slot(area(NL)) for _ in range(3)]
            GATE = area(NT)
            LI = [area(NT) for _ in range(2)]
            LF = [area(NT) for _ in range(2)]
            MM = area(2 * NL)
            GT = area(96).rearrange("p (d b h) -> p d b h", d=2, b=6)
            MD = area(NL)
            MB = area(NL)
            CM = area(256 + 1024)
            HF = area(NL)
            FL = area(NL)
            SC2 = GATE[:, 0:NL]
            free = state["arena_free"]
            co = CONST_AT["mask_f"][0]
            t_cm = fetch(CM, consts[:, co:co + 1280], free)
            masks = [CM[:, 0:128], CM[:, 128:256]]
            selm = CM[:, 256:1280].rearrange("p (h n) -> p h n", h=8)
            layer = 1
            gain = lambda c: (lambda k: GS[:, layer, 0, k, c:c + 1])
            shift = lambda c: (lambda k: mod(layer, 0, k, c))
            th = norm_main(gain, shift, True, [t_mod[(1, 0)], t_mod[(1, 1)]])
            SC.wait(free)
            GP.wait(free)
            VE.wait(free)

            s, tl = load("ml_g", 0)
            w = s.ap[:, 0:1024].rearrange("p (k n) -> p k n", k=8)
            t_gate = []
            for h, n, tk, off in ((H, NL, th[0], NC), (HC, NC, th[1], 0)):
                b = bank()
                t = mm_group(b.ap[:, 0:n], [(w[:, k, :], h[:, k, :]) for k in range(8)], [tl, tk, b.free])
                s.free = [t]
                SC.wait(t)
                t = SC.done(sc.activation(GATE[:, off:off + n], b.ap[:, 0:n], ACT.Identity, bias=vec("ml_gate_b")))
                b.free = [t]
                t_gate.append(t)
            t_f = []
            t_i = []
            for d in range(2):
                r0 = 64 * d
                VE.wait(t_gate)
                t_i.append(VE.done(ve.tensor_copy(LI[d][0:8, :], GATE[r0:r0 + 8, :])))
                t1 = VE.done(ve.tensor_copy(LF[d][0:8, :], GATE[r0 + 32:r0 + 40, :]))
                t_f.append(t1)
            W = [PP[0].ap, PP[1].ap, PP[2].ap, PP[3].ap]
            lf_done = []
            for d in range(2):
                tt = []
                for c0, n in ((0, NC), (NC, NL)):
                    a = (W[0] if n == NC else W[1])[32 * 0:8, 0:n]
                    f = LF[d][0:8, c0:c0 + n]
                    SC.wait(t_f[d], lf_done)
                    t = SC.done(sc.activation(a, f, ACT.Abs))
                    SC.wait(t)
                    t = SC.done(sc.activation(a, a, ACT.Exp, scale=-1.0))
                    SC.wait(t)
                    t = SC.done(sc.activation(a, a, ACT.Ln, bias=1.0))
                    VE.wait(t, t_f[d])
                    tt.append(VE.done(ve.scalar_tensor_tensor(out=f, in0=f, scalar=0.0, in1=a, op0=ALU.min,
                                                              op1=ALU.subtract)))
                lf_done = tt
                t_f[d] = tt
            one8 = W[2]
            t1 = VE.done(ve.memset(one8[0:8, :], 1.0))
            t_dir = []
            for d in range(2):
                F = LF[d]
                VE.wait(t1, t_f[d], t_i[d])
                if d == 0:
                    t = VE.done(ve.tensor_tensor_scan(F[0:8, 0:NC], one8[0:8, 0:NC], F[0:8, 0:NC], 0.0,
                                                      ALU.mult, ALU.add))
                    VE.wait(t)
                    t = VE.done(ve.tensor_tensor_scan(F[0:8, NC:NT], one8[0:8, :], F[0:8, NC:NT],
                                                      F[0:8, NC - 1:NC], ALU.mult, ALU.add))
                else:
                    t = VE.done(ve.tensor_tensor_scan(F[0:8, 0:NC][:, ::-1], one8[0:8, 0:NC], F[0:8, 0:NC][:, ::-1],
                                                      0.0, ALU.mult, ALU.add))
                    VE.wait(t)
                    t = VE.done(ve.tensor_tensor_scan(F[0:8, NC:NT][:, ::-1], one8[0:8, :], F[0:8, NC:NT][:, ::-1],
                                                      F[0:8, 0:1], ALU.mult, ALU.add))
                VE.wait(t)
                G = LI[d]
                t = VE.done(ve.tensor_tensor(G[0:8, :], G[0:8, :], F[0:8, :], ALU.subtract))
                VE.wait(t)
                mx = SM[0:8, 16 + d:17 + d]
                t = VE.done(ve.tensor_reduce(mx, G[0:8, 0:NC], AX.X, ALU.max))
                VE.wait(t)
                t = VE.done(ve.tensor_scalar(mx, mx, 0.0, None, ALU.max))
                VE.wait(t)
                M = MM[0:8, NL * d:NL * d + NL]
                gl = G[0:8, NC:NT]
                if d == 0:
                    t = VE.done(ve.tensor_tensor_scan(M, gl, gl, mx, ALU.max, ALU.max))
                else:
                    t = VE.done(ve.tensor_tensor_scan(M[:, ::-1], gl[:, ::-1], gl[:, ::-1], mx, ALU.max, ALU.max))
                VE.wait(t)
                t = VE.done(ve.tensor_tensor(F[0:8, NC:NT], F[0:8, NC:NT], M, ALU.add))
                t2 = VE.done(ve.tensor_scalar(M, M, -1.0, None, ALU.mult))
                SC.wait(t)
                t = SC.done(sc.activation(F[0:8, NC:NT], F[0:8, NC:NT], ACT.Exp, scale=-1.0))
                t_dir.append([t, t2])
            b = bank()
            PE.wait(t_dir, b.free)
            for d in range(2):
                for kb in range(6):
                    c = (d * 6 + kb) * 8
                    ins = pe.transpose(b.ap[:, c:c + 8], LI[d][0:8, kb * 128:(kb + 1) * 128], ident[0:8, 0:8])
            t = PE.done(ins)
            VE.wait(t)
            t_gt = VE.done(ve.tensor_copy(GT[:, :, :, :].rearrange("p d b h -> p (d b h)"), b.ap[:, 0:96]))
            b.free = [t_gt]

            t_qk = []
            wo = VEC_AT["ml_conv_w"][0]
            bo = VEC_AT["ml_conv_b"][0]
            for m in range(8):
                s, tl = load("ml_qk", m)
                w = s.ap[:, 0:1024].rearrange("p (k n) -> p k n", k=8)
                ts = []
                for h, n, tk, off in ((H, NL, th[0], NC), (HC, NC, th[1], 0))[0:1 if m < 4 else 2]:
                    b = bank()
                    t = mm_group(b.ap[:, 0:n], [(w[:, k, :], h[:, k, :]) for k in range(8)], [tl, tk, b.free])
                    s.free = [t]
                    dst = QQ[:, m, :] if m < 4 else KK[:, m - 4, off:off + n]
                    gv = b.ap[:, 0:n]
                    SC.wait(t)
                    t = SC.done(sc.activation(dst, gv, ACT.Identity, bias=VEC[:, bo + m:bo + m + 1],
                                              scale=VEC[:, wo + 8 + m:wo + 9 + m]))
                    VE.wait(t)
                    t = VE.done(ve.scalar_tensor_tensor(out=dst[:, 1:n], in0=gv[:, 0:n - 1],
                                                        scalar=VEC[:, wo + m:wo + m + 1], in1=dst[:, 1:n],
                                                        op0=ALU.mult, op1=ALU.add))
                    VE.wait(t)
                    t = VE.done(ve.scalar_tensor_tensor(out=dst[:, 0:n - 1], in0=gv[:, 1:n],
                                                        scalar=VEC[:, wo + 16 + m:wo + 17 + m], in1=dst[:, 0:n - 1],
                                                        op0=ALU.mult, op1=ALU.add))
                    b.free = [t]
                    SC.wait(t)
                    t = SC.done(sc.activation(dst, dst, ACT.Silu))
                    ts.append(t)
                t_qk.append(ts)
            t_v = []
            for c in range(4):
                s, tl = load("ml_v", c)
                w = s.ap.rearrange("p (k n) -> p k n", k=8)
                for tb in range(6):
                    hb = (lambda k: HC[:, k, tb * 128:(tb + 1) * 128]) if tb < 2 else \
                        (lambda k: H[:, k, (tb - 2) * 128:(tb - 1) * 128])
                    b = bank()
                    t = mm_group(b.ap[:, 0:256], [(hb(k), w[:, k, :]) for k in range(8)], [tl, b.free])
                    s.free = [t]
                    VE.wait(t)
                    t = VE.done(ve.tensor_copy(V[:, tb, c * 256:(c + 1) * 256], b.ap[:, 0:256]))
                    b.free = [t]
                t_v.append(t)
            t_o = []
            for m in range(8):
                s, tl = load("ml_o", m)
                w = s.ap[:, 0:1024].rearrange("p (k n) -> p k n", k=8)
                b = bank()
                t = mm_group(b.ap[:, 0:NL], [(w[:, k, :], H[:, k, :]) for k in range(8)], [tl, b.free])
                s.free = [t]
                t_hlast = t
                SC.wait(t)
                t = SC.done(sc.activation(O[:, m, :], b.ap[:, 0:NL], ACT.Sigmoid))
                b.free = [t]
                t_o.append(t)

            prot = Rotor(PP)
            drot = Rotor(DD)
            for p in PP:
                p.free = [t_dir, t1]
            mb_free, md_free, fl_free = [], [], []
            t_mix = []
            hf_free = []
            for h in range(8):
                rows = slice(64 * (h % 2), 64 * (h % 2) + 64)
                t_in = [t_qk[h // 2], t_qk[4 + h // 2]]
                t_h = None
                for d in range(2):
                    b = bank()
                    t = mm_group(b.ap[:, 0:NL], [(selm[0:8, h, :], MM[0:8, NL * d:NL * d + NL])], [t_cm, t_dir, b.free])
                    SC.wait(t, mb_free)
                    t_mb = SC.done(sc.activation(MB, b.ap[:, 0:NL], ACT.Copy))
                    VE.wait(t_mb, md_free)
                    t_md = VE.done(ve.tensor_tensor(
                        MD.rearrange("p (b n) -> p b n", b=4), MB.rearrange("p (b n) -> p b n", b=4),
                        masks[d].unsqueeze(1).broadcast_to([P, 4, 128]), ALU.add))
                    b.free = [t_mb]
                    ps_list = []
                    for kb in range(6):
                        if kb < 2:
                            spans = [(MB, 0, NL)]
                        else:
                            j = kb - 2
                            lo, hi = 128 * j, 128 * j + 128
                            spans = [(MD, lo, hi)]
                            if d == 0 and hi < NL:
                                spans.append((MB, hi, NL))
                            if d == 1 and lo > 0:
                                spans.append((MB, 0, lo))
                        q0 = min(x[1] for x in spans)
                        q1 = max(x[2] for x in spans)
                        bs = bank()
                        tS = mm_group(bs.ap[:, q0:q1], [(KK[rows, h // 2, kb * 128:(kb + 1) * 128],
                                                         QQ[rows, h // 2, q0:q1])], [t_in, bs.free])
                        dd = drot.take()
                        SC.wait(t_gt, t_md, dd.free)
                        for src, lo, hi in spans:
                            tD = SC.done(sc.activation(dd.ap[:, lo:hi], src[:, lo:hi], ACT.Exp,
                                                       bias=GT[:, d, kb, h:h + 1]))
                        mb_free = [tD]
                        md_free = [tD]
                        pp = prot.take()
                        VE.wait(tS, tD, pp.free)
                        t = VE.done(ve.scalar_tensor_tensor(out=pp.ap[:, q0:q1], in0=bs.ap[:, q0:q1], scalar=0.125,
                                                            in1=dd.ap[:, q0:q1], op0=ALU.mult, op1=ALU.mult))
                        dd.free = [t]
                        bs.free = [t]
                        ps_list.append((pp, kb, q0, q1, t))
                    bn, bd = bank(), bank()
                    PE.wait(bn.free, bd.free, t_v)
                    for i, (pp, kb, q0, q1, t) in enumerate(ps_list):
                        PE.wait(t)
                        pe.matmul(bn.ap[:, q0:q1], V[:, kb, h * 128:(h + 1) * 128], pp.ap[:, q0:q1],
                                  start=(i == 0), stop=(i == 5), skip_group_check=True)
                        ins = pe.matmul(bd.ap[:, q0:q1], ones, pp.ap[:, q0:q1],
                                        start=(i == 0), stop=(i == 5), skip_group_check=True)
                        tp = PE.done(ins)
                        pp.free = [tp]
                    bf = bank()
                    tf = mm_group(bf.ap[:, 0:NL], [(selm[0:8, h, :], LF[d][0:8, NC:NT])], [bf.free])
                    SC.wait(tp, fl_free)
                    t = SC.done(sc.activation(FL, bd.ap[:, 0:NL], ACT.Abs))
                    bd.free = [t]
                    VE.wait(t, tf)
                    t = VE.done(ve.tensor_tensor(FL, bf.ap[:, 0:NL], FL, ALU.max))
                    bf.free = [t]
                    VE.wait(t)
                    t = VE.done(ve.reciprocal(FL, FL))
                    VE.wait(t, hf_free if d == 0 else None)
                    dst = HF if d == 0 else SC2
                    t = VE.done(ve.tensor_tensor(dst, bn.ap[:, 0:NL], FL, ALU.mult))
                    bn.free = [t]
                    fl_free = [t]
                    t_h = t
                VE.wait(t_h)
                t = VE.done(ve.tensor_tensor(HF, HF, SC2, ALU.add))
                s = tmp.take()
                SC.wait(t, s.free)
                t2 = SC.done(sc.activation(s.ap, HF, ACT.Square))
                b = bank()
                tq = mm_group(b.ap[:, 0:NL], [(ones, s.ap)], [t2, b.free])
                s.free = [tq]
                VE.wait(hf_free)
                tr = rstd_of(b, slice(0, P), NL, 128, EPS, SC2, tq)
                VE.wait(tr)
                t = VE.done(ve.scalar_tensor_tensor(out=HF, in0=HF, scalar=vec("ml_out_g", h), in1=SC2,
                                                    op0=ALU.mult, op1=ALU.mult))
                VE.wait(t, t_o[h], t_hlast)
                t = VE.done(ve.tensor_tensor(H[:, h, :], HF, O[:, h, :], ALU.mult))
                hf_free = [t]
                t_mix.append(t)
            t = project_out("ml_out", lambda si, k: H[:, k, :], [(0, NL)], t_mix,
                            lambda m, si: mod(1, 2, m, 0), t_mod[(1, 2)])
            state["h_free"] = [t]
            state["arena_free"] = [t]

        def recurrent():
            o = [0]

            def area(n):
                o[0] += n
                assert o[0] <= ARENA, o[0]
                return A[:, o[0] - n:o[0]]

            def tiles(n=8):
                return area(n * NL).rearrange("p (h t) -> p h t", h=n)

            GATE = tiles()
            REC = tiles()
            BX = tiles()
            AA = tiles()
            MU = tiles()
            free = state["arena_free"]
            th = norm_main(lambda c: (lambda k: vec("mix_norm_2", k)), None, False, [])[0]
            SC.wait(free)
            GP.wait(free)
            VE.wait(free)
            wo = VEC_AT["rec_conv_w_2"][0]
            bo = VEC_AT["rec_conv_b_2"][0]
            t_gate, t_rec = [], []
            for c in range(8):
                s, tl = load("rec_in", c)
                w = s.ap.rearrange("p (k n) -> p k n", k=8)
                for j in range(2):
                    m = 2 * c + j
                    b = bank()
                    t = mm_group(b.ap[:, 0:NL], [(w[:, k, j * 128:(j + 1) * 128], H[:, k, :]) for k in range(8)],
                                 [tl, th, b.free])
                    SC.wait(t)
                    if m < 8:
                        t = SC.done(sc.activation(GATE[:, m, :], b.ap[:, 0:NL], ACT.Gelu_apprx_tanh))
                        b.free = [t]
                        t_gate.append(t)
                    else:
                        m -= 8
                        r = REC[:, m, :]
                        t = SC.done(sc.activation(r, b.ap[:, 0:NL], ACT.Identity, bias=VEC[:, bo + m:bo + m + 1],
                                                  scale=VEC[:, wo + 24 + m:wo + 25 + m]))
                        for q in range(3):
                            sh = 3 - q
                            VE.wait(t)
                            t = VE.done(ve.scalar_tensor_tensor(out=r[:, sh:NL], in0=b.ap[:, 0:NL - sh],
                                                                scalar=VEC[:, wo + 8 * q + m:wo + 8 * q + m + 1],
                                                                in1=r[:, sh:NL], op0=ALU.mult, op1=ALU.add))
                        b.free = [t]
                        t_rec.append(t)
                s.free = [(PE.sem, PE.n, id(PE))]
            state["h_free"] = [(PE.sem, PE.n, id(PE))]
            lo = VEC_AT["rec_lambda_2"][0]
            lam = VEC[:, lo:lo + 8]
            z, u, v, acc = SM[:, 32:40], SM[:, 40:48], SM[:, 48:56], SM[:, 56:64]
            t = SC.done(sc.activation(z, lam, ACT.Abs))
            SC.wait(t)
            t = SC.done(sc.activation(z, z, ACT.Exp, scale=-1.0))

            def step(ins):
                t = VE.done(ins)
                VE.wait(t)
                return t

            VE.wait(t)
            step(ve.tensor_scalar(u, z, 2.0, None, ALU.add))
            step(ve.reciprocal(u, u))
            step(ve.tensor_tensor(u, z, u, ALU.mult))
            step(ve.tensor_tensor(v, u, u, ALU.mult))
            step(ve.memset(acc, 1.0 / 19))
            for q in range(8, -1, -1):
                step(ve.tensor_tensor(acc, acc, v, ALU.mult))
                step(ve.tensor_scalar(acc, acc, 1.0 / (2 * q + 1), None, ALU.add))
            step(ve.tensor_tensor(acc, acc, u, ALU.mult))
            step(ve.tensor_scalar(u, lam, -1.0, 0.0, ALU.mult, ALU.max))
            step(ve.scalar_tensor_tensor(out=acc, in0=acc, scalar=2.0, in1=u, op0=ALU.mult, op1=ALU.add))
            step(ve.tensor_scalar(acc, acc, 8.0, None, ALU.mult))
            t_sp = step(ve.tensor_scalar(u, acc, -1.0, None, ALU.mult))
            SC.wait(t_sp)
            s, tl = load("rec_g", 0)
            w = s.ap.rearrange("p (g m n) -> p g m n", g=2, m=8)
            t_ri = []
            for m in range(8):
                pair = []
                for g, dst, name in ((0, AA, "rec_b_a_2"), (1, BX, "rec_b_x_2")):
                    b = bank()
                    t = mm_group(b.ap[:, 0:NL], [(w[:, g, m, :], REC[:, m, :])], [tl, t_rec[m], b.free])
                    SC.wait(t)
                    t = SC.done(sc.activation(dst[:, m, :], b.ap[:, 0:NL], ACT.Sigmoid, bias=vec(name, m)))
                    b.free = [t]
                    pair.append(t)
                t_ri.append(pair)
            s.free = [(PE.sem, PE.n, id(PE))]
            t_a, t_m2 = [], []
            for m in range(8):
                SC.wait(t_ri[m])
                tT = SC.done(sc.activation(MU[:, m, :], AA[:, m, :], ACT.Tanh, scale=acc[:, m:m + 1]))
                t_a.append(SC.done(sc.activation(AA[:, m, :], AA[:, m, :], ACT.Exp, scale=u[:, m:m + 1])))
                VE.wait(tT)
                q = tmp.take()
                VE.wait(q.free)
                step(ve.tensor_scalar(q.ap, MU[:, m, :], 1.0, None, ALU.add))
                step(ve.reciprocal(q.ap, q.ap))
                t = VE.done(ve.scalar_tensor_tensor(out=MU[:, m, :], in0=MU[:, m, :], scalar=2.0, in1=q.ap,
                                                    op0=ALU.mult, op1=ALU.mult))
                q.free = [t]
                t_m2.append(t)
            SC.wait(t_m2)
            t_out = []
            for m in range(8):
                tq = SC.done(sc.activation(MU[:, m, :], MU[:, m, :], ACT.Sqrt))
                GP.wait(t_ri[m], t_rec[m])
                tg = GP.done(gp.tensor_tensor(BX[:, m, :], BX[:, m, :], REC[:, m, :], ALU.mult))
                VE.wait(tq, tg)
                t = VE.done(ve.tensor_tensor(BX[:, m, :], BX[:, m, :], MU[:, m, :], ALU.mult))
                VE.wait(t, t_a[m])
                t = VE.done(ve.tensor_tensor_scan(REC[:, m, :], AA[:, m, :], BX[:, m, :], 0.0, ALU.mult, ALU.add))
                VE.wait(t, t_gate[m])
                t_out.append(VE.done(ve.tensor_tensor(GATE[:, m, :], GATE[:, m, :], REC[:, m, :], ALU.mult)))
            t = project_out("rec_out", lambda si, k: GATE[:, k, :], [(0, NL)], t_out, lambda m, si: 1.0, None)
            state["arena_free"] = [t]

        KS_OFF = FT * NL
        KS = A[:, KS_OFF:KS_OFF + 16 * NL].rearrange("p (h t) -> p h t", h=16)
        VS = A[:, KS_OFF + 16 * NL:KS_OFF + 24 * NL].rearrange("p (b n) -> p b n", b=4)
        shared = {}

        def qk_tile(b, tb, gain, dst0, dst1, R2, rot2, t_r2, deps):
            s = tmp.take()
            SC.wait(tb, s.free)
            t = SC.done(sc.activation(s.ap, b.ap[:, 0:NL], ACT.Square))
            b2 = bank()
            tq = mm_group(b2.ap[:, 0:NL], [(bones, s.ap)], [t, b2.free])
            s.free = [tq]
            r = tmp.take()
            VE.wait(r.free)
            t = rstd_of(b2, slice(0, P), NL, 64, EPS, r.ap, tq)
            q = tmp.take()
            VE.wait(t, q.free, tb)
            t = VE.done(ve.scalar_tensor_tensor(out=q.ap, in0=b.ap[:, 0:NL], scalar=gain, in1=r.ap,
                                                op0=ALU.mult, op1=ALU.mult))
            r.free = [t]
            b.free = [t]
            b3 = bank()
            tr = mm_group(b3.ap[:, 0:NL], [(rot2, q.ap)], [t, t_r2, b3.free])
            u = tmp.take()
            VE.wait(tr, u.free)
            t1 = VE.done(ve.tensor_tensor(u.ap, b3.ap[:, 0:NL], R2[:, 512:1024], ALU.mult))
            b3.free = [t1]
            t2 = VE.done(ve.tensor_tensor(q.ap, q.ap, R2[:, 0:512], ALU.mult))
            VE.wait(t1, t2, *deps)
            for half, dst in ((0, dst0), (64, dst1)):
                t = VE.done(ve.tensor_tensor(dst, q.ap[half:half + 64, :], u.ap[half:half + 64, :], ALU.add))
            q.free = [t]
            u.free = [t]
            return t

        def rope2(off, free):
            R2 = A[:, off:off + 1024]
            rot = A[:, off + 1024:off + 1152]
            t = [fetch(R2, const("rope_2"), free), fetch(rot, const("rot_2"), free)]
            return R2, rot, t

        def shared_kv():
            free = state["arena_free"]
            R2, rot2, t_r2 = rope2(0, free)
            VE.wait(t_r2)
            th = norm_main(lambda c: (lambda k: vec("kv_norm_2", k)), None, False, [])[0]
            VE.wait(free)
            SC.wait(free)
            GP.wait(free)
            t_k = []
            for c in range(4):
                s, tl = load("wk", c)
                w = s.ap.rearrange("p (k n) -> p k n", k=8)
                for j in range(2):
                    h = 2 * c + j
                    b = bank()
                    tb = mm_group(b.ap[:, 0:NL], [(w[:, k, j * 128:(j + 1) * 128], H[:, k, :]) for k in range(8)],
                                  [tl, th, b.free])
                    s.free = [tb]
                    t_k.append(qk_tile(b, tb, vec("k_norm_2"), KS[0:64, 2 * h, :], KS[0:64, 2 * h + 1, :], R2, rot2,
                                       t_r2, []))
            t_one = GP.done(gp.memset(KS[64:65, :, :], 1.0))
            t_v = []
            for c in range(4):
                s, tl = load("wv", c)
                w = s.ap.rearrange("p (k n) -> p k n", k=8)
                for tb in range(4):
                    b = bank()
                    t = mm_group(b.ap[:, 0:256], [(H[:, k, tb * 128:(tb + 1) * 128], w[:, k, :]) for k in range(8)],
                                 [tl, b.free])
                    s.free = [t]
                    state["h_free"] = [t]
                    SC.wait(t)
                    t = SC.done(sc.activation(VS[:, tb, c * 256:(c + 1) * 256], b.ap[:, 0:256], ACT.Copy))
                    b.free = [t]
                t_v.append(t)
            shared.update(k=t_k, v=t_v, one=t_one)
            state["arena_free"] = [(PE.sem, PE.n, id(PE)), (VE.sem, VE.n, id(VE))]

        def diff_attention():
            o = [0]

            def area(n):
                o[0] += n
                assert o[0] <= KS_OFF, o[0]
                return A[:, o[0] - n:o[0]]

            MIX = A[:, KS_OFF + 24 * NL:KS_OFF + 32 * NL].rearrange("p (h t) -> p h t", h=8)
            SSQ = XC[:, :, :].rearrange("p (a b) t -> p a (b t)", a=4)
            free = state["arena_free"]
            R2, rot2, t_r2 = rope2(0, free)
            area(1152)
            Q = area(8 * NL).rearrange("p (h t) -> p h t", h=8)
            PR = [Slot(area(NL)) for _ in range(8)]
            O0 = area(NL)
            O1 = area(NL)
            VE.wait(t_r2)
            th = norm_main(lambda c: (lambda k: vec("mix_norm_2", 8 + k)), None, False, [])[0]
            VE.wait(free)
            SC.wait(free)
            GP.wait(free)
            LM = SM[:, 64:72]
            VE.wait(t_eps)
            cols = [VEC_AT[x][0] for x in ("lambda_q1_2", "lambda_q2_2", "lambda_k1_2", "lambda_k2_2")]
            t = VE.done(ve.tensor_tensor(LM[0:64, 0:2], VEC[0:64, cols[0]:cols[0] + 2],
                                         VEC[0:64, cols[2]:cols[2] + 2], ALU.mult))
            b = bank()
            t = mm_group(b.ap[:, 0:2], [(ones[0:64, :], LM[0:64, 0:2])], [t, b.free])
            SC.wait(t)
            t = SC.done(sc.activation(LM[:, 2:4], b.ap[:, 0:2], ACT.Exp))
            b.free = [t]
            VE.wait(t)
            t = VE.done(ve.tensor_tensor(LM[:, 4:5], LM[:, 3:4], LM[:, 2:3], ALU.subtract))
            VE.wait(t)
            t = VE.done(ve.tensor_scalar(LM[:, 4:5], LM[:, 4:5], -LAMBDA_INIT, None, ALU.add))
            t2 = VE.done(ve.tensor_scalar(LM[:, 5:6], vec("q_norm_2"), 0.125, None, ALU.mult))
            t3 = VE.done(ve.tensor_scalar(LM[:, 6:7], vec("sub_norm_2"), 1.0 - LAMBDA_INIT, None, ALU.mult))
            VE.wait(t, t2, t3)
            neg_lam, q_gain, o_gain = LM[:, 4:5], LM[:, 5:6], LM[:, 6:7]
            t_mix = []
            t_hq = [None]
            q_free = [[], []]
            o_free = [[]]
            slots_w = {}

            def query(c, j):
                h = 2 * c + j
                if j == 0:
                    slots_w[c] = load("wq", c)
                s, tl = slots_w[c]
                w = s.ap.rearrange("p (k n) -> p k n", k=8)
                b = bank()
                tb = mm_group(b.ap[:, 0:NL], [(w[:, k, j * 128:(j + 1) * 128], H[:, k, :]) for k in range(8)],
                              [tl, th, b.free])
                s.free = [tb]
                t_hq[0] = tb
                return qk_tile(b, tb, q_gain, Q[0:64, 2 * (h % 4), :], Q[0:64, 2 * (h % 4) + 1, :], R2, rot2,
                               t_r2, [q_free[h // 4 % 2]] if h >= 4 else [])

            for half in range(2):
                t_q = []
                for c in (2 * half, 2 * half + 1):
                    for j in range(2):
                        t_q.append(query(c, j))
                jobs = []
                for hh in range(4):
                    h = 4 * half + hh
                    for comp in range(2):
                        def finish(outs, h=h, comp=comp):
                            (bo_, to), (bs_, ts) = outs
                            r = tmp.take()
                            VE.wait(ts, r.free)
                            t = VE.done(ve.reciprocal(r.ap, bs_.ap[:, 0:NL]))
                            bs_.free = [t]
                            VE.wait(t, o_free[0])
                            dst = (O0, O1)[comp]
                            t = VE.done(ve.tensor_tensor(dst, bo_.ap[:, 0:NL], r.ap, ALU.mult))
                            bo_.free = [t]
                            r.free = [t]
                            if comp == 0:
                                o_free[0] = []
                                return
                            VE.wait(t)
                            t = VE.done(ve.scalar_tensor_tensor(out=O0, in0=O1, scalar=neg_lam, in1=O0,
                                                                op0=ALU.mult, op1=ALU.add))
                            VE.wait(t)
                            s = tmp.take()
                            VE.wait(s.free)
                            t = VE.done(ve.tensor_tensor(s.ap, O0, O0, ALU.mult))
                            b = bank()
                            tq = mm_group(b.ap[:, 0:NL], [(ones, s.ap)], [t, b.free])
                            s.free = [tq]
                            t = VE.done(ve.tensor_scalar(MIX[:, h, :], O0, o_gain, None, ALU.mult))
                            o_free[0] = [t]
                            SC.wait(tq)
                            t2 = SC.done(sc.activation(SSQ[:, h % 4, :], b.ap[:, 0:NL], ACT.Copy))
                            b.free = [t2]
                            t_mix.append((t, t2))

                        jobs.append(dict(
                            d=64, scale=1.0, q=Q[:, 2 * hh + comp, :], k=KS[:, 2 * h + comp, :], nq=NL, nk=NL, causal=True,
                            deps=[t_q[hh], shared["k"][h]], t_one=shared["one"], t_v=shared["v"],
                            v=[lambda kb, h=h: VS[:, kb, h * 128:(h + 1) * 128], lambda kb: ones], finish=finish))
                attention(jobs, PR)
                q_free[0] = [(PE.sem, PE.n, id(PE))]
                q_free[1] = q_free[0]
                for hh in range(4):
                    h = 4 * half + hh
                    SC.wait(t_mix[h][1])
                    t = SC.done(sc.activation(SSQ[:, hh, :], SSQ[:, hh, :], ACT.Sqrt, bias=eps_ap(SUB_EPS),
                                              scale=1.0 / 128))
                    VE.wait(t)
                    t = VE.done(ve.reciprocal(SSQ[:, hh, :], SSQ[:, hh, :]))
                    VE.wait(t, t_mix[h][0])
                    t = VE.done(ve.tensor_tensor(MIX[:, h, :], MIX[:, h, :], SSQ[:, hh, :], ALU.mult))
                    t_mix[h] = (t, t)
                    SC.wait(t)
            t = project_out("wo", lambda si, k: MIX[:, k, :], [(0, NL)], [list(x) for x in t_mix],
                            lambda m, si: 1.0, None)
            state["h_free"] = [t_hq[0], t]
            state["arena_free"] = [t]

        for i in range(8):
            ada_chunk(0, i)
        side.extend([lambda i=i: ada_chunk(0, i) for i in range(8, 24)])
        even_mixer()
        if stop > 1:
            side.extend([lambda i=i: ada_chunk(1, i) for i in range(24)])
            th = norm_main(lambda c: (lambda k: GS[:, 0, 1, k, c:c + 1]), lambda c: (lambda k: mod(0, 3, k, c)), True,
                           [t_mod[(0, 3)], t_mod[(0, 4)]])
            ffn("up0", "down0", th, True, 0, lambda m, si: mod(0, 5, m, si), t_mod[(0, 5)])
            run_side(99)
        if stop > 2:
            odd_mixer()
        if stop > 3:
            th = norm_main(lambda c: (lambda k: GS[:, 1, 1, k, c:c + 1]), lambda c: (lambda k: mod(1, 3, k, c)), False,
                           [t_mod[(1, 3)], t_mod[(1, 4)]])
            ffn("up1", "down1", th, False, 1, lambda m, si: mod(1, 5, m, si), t_mod[(1, 5)])
        if stop > 4:
            th = norm_main(lambda c: (lambda k: vec("ffn1_norm_2", k)), None, False, [])
            ffn("s_up10", "s_down10", th, False, None, lambda m, si: 0.5, None)
        if stop > 5:
            recurrent()
        if stop > 6:
            th = norm_main(lambda c: (lambda k: vec("ffn2_norm_2", k)), None, False, [])
            ffn("s_up20", "s_down20", th, False, None, lambda m, si: 0.5, None)
        if stop > 7:
            shared_kv()
            th = norm_main(lambda c: (lambda k: vec("ffn1_norm_2", 8 + k)), None, False, [])
            ffn("s_up11", "s_down11", th, False, None, lambda m, si: 0.5, None)
        if stop > 8:
            diff_attention()
        if stop > 9:
            th = norm_main(lambda c: (lambda k: vec("ffn2_norm_2", 8 + k)), None, False, [])
            ffn("s_up21", "s_down21", th, False, None, lambda m, si: 0.5, None)

        s_out = sem("s_out")
        out = outT.rearrange("(k p) t -> p k t", p=P)
        for m in range(KT):
            sp_wait(state["x"][m])
            nc.sync.dma_start(out[:, m, :], X[:, m, :]).then_inc(s_out, 16)
        nc.sync.wait_ge(s_out, 16 * KT)


def _columns(w, n):
    k = w.shape[0] // P
    return w.reshape(k, P, w.shape[1] // n, n).transpose(2, 1, 0, 3)


def _up(gate, val):
    return np.stack([_columns(gate, 128), _columns(val, 128)], 2)


def _down(w):
    t = w.reshape(FT, P, 4, 256).transpose(2, 1, 0, 3)
    return np.concatenate([t[m, :, k:min(k + 8, FT)].reshape(-1) for m in range(4) for k in (0, 8, 16)])


def _layout(i):
    w = {}
    for l in range(2):
        w[f"ada{l}"] = _columns(i["ada_w"][l], 256)
        w[f"up{l}"] = _up(i["ffn_w_up"][l][:, :2816], i["ffn_w_up"][l][:, 2816:])
        w[f"down{l}"] = _down(i["ffn_w_down"][l])
        for f in (1, 2):
            w[f"s_up{f}{l}"] = _up(i[f"ffn{f}_w_gate_2"][l], i[f"ffn{f}_w_up_2"][l])
            w[f"s_down{f}{l}"] = _down(i[f"ffn{f}_w_down_2"][l])
    a = i["att_w_in"][0]
    w["att_cq"] = _columns(a[:, 0:384], 128)
    w["att_ckv"] = _columns(a[:, 384:640], 128)
    w["att_kr"] = _columns(a[:, 640:672], 32)
    w["att_gq"] = _columns(a[:, 672:1184], 128)
    w["att_gk"] = _columns(a[:, 1184:1312], 128)
    w["att_gv"] = _columns(a[:, 1312:1440], 128)
    w["qb"] = i["mla_w_qb"][0].reshape(3, P, 2, 4, 96).transpose(2, 1, 3, 0, 4)
    kv = i["mla_w_kvb"][0].reshape(2, P, 8, 128)
    w["kb"] = kv[..., :64].transpose(1, 2, 0, 3)
    w["vb"] = kv[..., 64:].transpose(1, 0, 2, 3)
    w["att_out"] = _columns(i["att_w_out"][0], 256)
    m = i["ml_w_in"][0]
    w["ml_qk"] = _columns(m[:, 0:1024], 128)
    w["ml_v"] = _columns(m[:, 1024:2048], 256)
    w["ml_o"] = _columns(m[:, 2048:3072], 128)
    g = np.zeros((D, 4, 32), np.float32)
    g[:, :, 0:8] = m[:, 3072:3104].reshape(D, 4, 8)
    w["ml_g"] = _columns(g.reshape(D, 128), 128)
    w["ml_out"] = _columns(i["ml_w_out"][0], 256)
    w["rec_in"] = _columns(i["rec_w_in_2"][0], 256)
    w["rec_g"] = np.stack([i["rec_w_a_2"][0], i["rec_w_x_2"][0]]).transpose(2, 0, 1, 3)
    w["rec_out"] = _columns(i["rec_w_out_2"][0], 256)
    w["wk"] = _columns(i["w_k_2"], 256)
    w["wv"] = _columns(i["w_v_2"], 256)
    w["wq"] = _columns(i["attn_w_q_2"][0], 256)
    w["wo"] = _columns(i["attn_w_o_2"][0], 256)
    w = {k: np.ascontiguousarray(v).reshape(-1) for k, v in w.items()}

    vecs = np.zeros((P, NVEC), np.float32)
    for name, (o, n) in VEC_AT.items():
        v = i[name]
        if name in ("mla_q_g", "mla_k_g", "lambda_q1_2", "lambda_q2_2", "lambda_k1_2", "lambda_k2_2"):
            v = v.reshape(-1)
            vecs[0:v.size, o] = v
        elif name in ("gqa_q_g", "gqa_k_g", "k_norm_2", "q_norm_2"):
            vecs[0:64, o] = v.reshape(-1)
            vecs[64:128, o] = v.reshape(-1)
        elif name == "ml_gate_b":
            for q in range(4):
                vecs[32 * q:32 * q + 8, o] = v.reshape(4, 8)[q]
        else:
            vecs[:, o:o + n] = v.reshape(n, P).T
    return w, vecs


def _rope_axial(dim):
    rows = NL // 64
    row = np.repeat(np.arange(rows), 64).astype(np.float32)
    col = np.tile(np.arange(64), rows).astype(np.float32)
    nf = dim // 4
    inv = np.float32(10000.0) ** (-np.arange(nf, dtype=np.float32) / np.float32(nf))
    a, b = row[:, None] * inv, col[:, None] * inv
    ang = np.concatenate([a, a, b, b], axis=-1)
    return np.cos(ang).T, np.sin(ang).T


def _constants():
    c = np.zeros((P, NCONST), np.float32)

    def put(name, v):
        o, n = CONST_AT[name]
        c[:v.shape[0], o:o + v.shape[1]] = v

    put("ident", np.eye(P, dtype=np.float32))
    put("ones", np.ones((P, P), np.float32))
    put("bones", np.kron(np.eye(2), np.ones((64, 64))))

    def quarter(d):
        q = d // 4
        r = np.zeros((d, d))
        for i in range(q):
            r[i, q + i] = -1
            r[q + i, i] = 1
            r[2 * q + i, 3 * q + i] = -1
            r[3 * q + i, 2 * q + i] = 1
        return r.T

    def half(d):
        q = d // 2
        r = np.zeros((d, d))
        for i in range(q):
            r[i, q + i] = -1
            r[q + i, i] = 1
        return r.T

    put("rot_g", np.kron(np.eye(2), quarter(64)))
    rm = np.zeros((P, P))
    rm[64:96, 64:96] = quarter(32)
    put("rot_m", rm)
    put("rot_2", np.kron(np.eye(2), half(64)))
    s, t = np.arange(P)[:, None], np.arange(P)[None, :]
    put("mask_f", np.where(s <= t, 0.0, -1e30))
    put("mask_b", np.where(s >= t, 0.0, -1e30))
    sel = np.zeros((8, 8, P))
    for h in range(8):
        sel[h, h] = 1
    put("sel", sel.reshape(8, 1024))
    cm, sm = _rope_axial(32)
    rm = np.zeros((P, 1024))
    rm[64:96, 0:512], rm[64:96, 512:1024] = cm, sm
    put("rope_m", rm)
    cg, sg = _rope_axial(64)
    put("rope_g", np.concatenate([np.tile(cg, (2, 1)), np.tile(sg, (2, 1))], 1))
    pos = np.arange(NL, dtype=np.float32)
    inv = np.float32(10000.0) ** (-np.arange(0, 64, 2, dtype=np.float32) / np.float32(64))
    ang = pos[:, None] * inv[None, :]
    ang = np.concatenate([ang, ang], axis=-1)
    put("rope_2", np.concatenate([np.tile(np.cos(ang).T, (2, 1)), np.tile(np.sin(ang).T, (2, 1))], 1))
    return c


def _program(nc, arrays, stop=99):
    def given(name):
        a = arrays[name]
        return nc.dram_tensor(name, list(a.shape), F32, kind="ExternalInput").ap()

    out = nc.dram_tensor("outT", [D, NL], F32, kind="ExternalOutput").ap()
    weights = {name: given("w_" + name) for name in CHUNKS}
    build(nc, given("xT"), given("ctxT"), given("vecs"), given("consts"), weights, out, stop)


def _arrays(inputs):
    i = {k: np.asarray(v) for k, v in inputs.items()}
    w, vecs = _layout(i)
    arrays = {"w_" + k: v for k, v in w.items()}
    arrays["xT"] = np.ascontiguousarray(i["x"][0].T)
    arrays["ctxT"] = np.ascontiguousarray(i["ctx"][0].T)
    arrays["vecs"] = vecs
    arrays["consts"] = _constants()
    return arrays


def kernel(**inputs):
    import concourse.bacc as bacc
    from concourse.bass_utils import run_bass_kernel_spmd

    arrays = _arrays(inputs)
    nc = bacc.Bacc("TRN2", target_bir_lowering=False, num_devices=1)
    _program(nc, arrays)
    r = run_bass_kernel_spmd(nc, [arrays], core_ids=[0])
    return np.ascontiguousarray(r.results[0]["outT"].T).reshape(1, NL, D)
```

```python
from contextlib import ExitStack

import numpy as np
import concourse.bass as bass
from concourse import mybir

F32 = mybir.dt.float32
F32R = mybir.dt.float32r
ALU = mybir.AluOpType
ACT = mybir.ActivationFunctionType
AX = mybir.AxisListType

P = 128
D = 1024
KT = 8
NL = 512
NC = 256
NT = NC + NL
FT = 22
EPS = 1e-6
SUB_EPS = 1e-5
LAMBDA_INIT = 0.8 - 0.6 * float(np.exp(-0.3))
RING = 3
SLOT = 1024
HID = 10
GROUPS = ((0, 8), (8, 16), (16, 22))


def vec_columns():
    at, n = {}, 0
    for name, k in [
        ("c", 8), ("c_ctx", 8), ("ada_b", 96), ("norm1_g", 16), ("norm2_g", 16),
        ("ffn_conv_w", 132), ("ffn_conv_b", 44), ("mla_qa_g", 3), ("mla_kva_g", 2),
        ("mla_q_g", 1), ("mla_k_g", 1), ("gqa_q_g", 1), ("gqa_k_g", 1),
        ("ml_conv_w", 24), ("ml_conv_b", 8), ("ml_gate_b", 1), ("ml_out_g", 8),
        ("ffn1_norm_2", 16), ("ffn2_norm_2", 16), ("mix_norm_2", 16), ("rec_conv_w_2", 32),
        ("rec_conv_b_2", 8), ("rec_b_a_2", 8), ("rec_b_x_2", 8), ("rec_lambda_2", 8),
        ("kv_norm_2", 8), ("k_norm_2", 1), ("q_norm_2", 1), ("sub_norm_2", 1),
        ("lambda_q1_2", 1), ("lambda_q2_2", 1), ("lambda_k1_2", 1), ("lambda_k2_2", 1),
    ]:
        at[name] = (n, k)
        n += k
    return at, n


VEC_AT, NVEC = vec_columns()


def weight_chunks():
    down = [1024] * 16 + [768] * 8
    return {
        "ada0": [1024] * 48, "ada1": [1024] * 48,
        "up0": [1024] * 44, "down0": down, "up1": [1024] * 44, "down1": down,
        "att_in": [1024] * 12, "qb": [1152 // 2] * 4, "kb": [1024], "vb": [1024], "att_out": [1024] * 8,
        "ml_g": [1024], "ml_qk": [1024] * 8, "ml_v": [1024] * 8, "ml_o": [1024] * 8, "ml_out": [1024] * 8,
        "s_up10": [1024] * 44, "s_down10": down, "s_up20": [1024] * 44, "s_down20": down,
        "s_up11": [1024] * 44, "s_down11": down, "s_up21": [1024] * 44, "s_down21": down,
        "rec_in": [1024] * 16, "rec_g": [1024] * 2, "rec_out": [1024] * 8,
        "wk": [1024] * 8, "wv": [1024] * 8, "wq": [1024] * 8, "wo": [1024] * 8,
    }


CHUNKS = weight_chunks()

CONSTS = [("ident", 128), ("ones", 128), ("bones", 128), ("rot_g", 128), ("rot_m", 128), ("rot_2", 128),
          ("mask_f", 128), ("mask_b", 128), ("sel", 1024), ("rope_m", 1024), ("rope_g", 1024), ("rope_2", 1024)]


def const_columns():
    at, n = {}, 0
    for name, k in CONSTS:
        at[name] = (n, k)
        n += k
    return at, n


CONST_AT, NCONST = const_columns()


class Engine:

    def __init__(self, e, sem, serial=False):
        self.e, self.sem, self.n, self.seen, self.serial = e, sem, 0, {}, serial

    def wait(self, *tokens):
        for t in tokens:
            if t is None:
                continue
            if isinstance(t, list):
                self.wait(*t)
                continue
            sem, value, key = t
            if self.seen.get(key, 0) < value:
                self.seen[key] = value
                self.e.wait_ge(sem, value)

    def done(self, ins):
        self.n += 1
        ins.then_inc(self.sem, 1)
        token = (self.sem, self.n, id(self))
        if self.serial:
            self.wait(token)
        return token


class Slot:

    def __init__(self, ap):
        self.ap, self.free = ap, []


class Pair:

    def __init__(self, hi, lo):
        self.hi, self.lo = hi, lo

    def __getitem__(self, i):
        return Pair(self.hi[i], self.lo[i])


class Rotor:
    def __init__(self, slots):
        self.slots, self.i = slots, 0

    def take(self):
        s = self.slots[self.i % len(self.slots)]
        self.i += 1
        return s


def split_plan():
    order = []

    def whole(name):
        order.extend((name, i) for i in range(len(CHUNKS[name])))

    def feed(up, down):
        at = 0
        for g, (a, b) in enumerate(GROUPS):
            upto = min(b + 1, FT)
            order.extend((up, i) for i in range(2 * at, 2 * upto))
            at = upto
            order.extend((down, 8 * g + m) for m in range(8))

    whole("att_in")
    whole("att_out")
    feed("up0", "down0")
    for name in ("ml_g", "ml_qk", "ml_v", "ml_o", "ml_out"):
        whole(name)
    feed("up1", "down1")
    feed("s_up10", "s_down10")
    order.extend(("rec_in", i) for i in (*range(8, 16), *range(8)))
    whole("rec_out")
    feed("s_up20", "s_down20")
    whole("wk")
    whole("wv")
    feed("s_up11", "s_down11")
    whole("wq")
    whole("wo")
    feed("s_up21", "s_down21")
    return order


def build(nc, xT, ctxT, vecs, consts, weights, outT):
    with ExitStack() as ctx:
        names = [0]

        def alloc(scope, *shape, dt=F32):
            names[0] += 1
            return scope.enter_context(nc.sbuf_tensor(f"t{names[0]}", [P, *shape], dt))

        def alloc_pair(scope, *shape):
            return Pair(alloc(scope, *shape, dt=F32R), alloc(scope, *shape, dt=F32R))

        def sem(name):
            return ctx.enter_context(nc.semaphore(name))

        PE = Engine(nc.tensor, sem("s_pe"))
        VE = Engine(nc.vector, sem("s_ve"))
        SC = Engine(nc.scalar, sem("s_sc"))
        GP = Engine(nc.gpsimd, sem("s_gp"), serial=True)
        pe, ve, sc, gp = PE.e, VE.e, SC.e, GP.e

        X = alloc(ctx, KT, NL)
        XC = alloc(ctx, KT, NC)
        VEC = alloc(ctx, NVEC)
        MOD = alloc(ctx, 2, 48, 2)
        GS = alloc(ctx, 2, 2, 8, 2)
        CS = alloc(ctx, 8, 2)
        RS = alloc(ctx, NT)
        MN = alloc(ctx, 8, 8)
        CONST = alloc(ctx, 384)
        SM = alloc(ctx, 128)
        TMP = alloc(ctx, 4, NL)
        raw_t = alloc(ctx, RING, SLOT)
        hi_t = alloc(ctx, RING, SLOT, dt=F32R)
        lo_t = alloc(ctx, RING, SLOT, dt=F32R)
        ps = ctx.enter_context(nc.psum_tensor("ps", [P, 8, 512], F32))

        banks = [Slot(ps[:, i, :]) for i in range(8)]
        brot = [0]
        bank_turns = [7]

        def bank():
            brot[0] = (brot[0] + 1) % bank_turns[0]
            return banks[brot[0]]

        tmp = Rotor([Slot(TMP[:, i, :]) for i in range(4)])

        raws = Rotor([Slot(raw_t[:, i, :]) for i in range(RING)])
        raw_sem = [sem(f"s_w{i}") for i in range(RING)]
        pairs = Rotor([Slot(Pair(hi_t[:, i, :], lo_t[:, i, :])) for i in range(RING)])
        offsets = {}
        for name, sizes in CHUNKS.items():
            o = [0]
            for f in sizes:
                o.append(o[-1] + f * P)
            offsets[name] = o
        sp_seen = {}

        def sp_wait(t):
            if isinstance(t, list):
                for x in t:
                    sp_wait(x)
                return
            s, value, key = t
            if sp_seen.get(key, 0) < value:
                sp_seen[key] = value
                nc.sync.wait_ge(s, value)

        def load(name, i):
            k = raws.i % RING
            turn = raws.i // RING + 1
            s = raws.take()
            sp_wait(s.free)
            f = CHUNKS[name][i]
            o = offsets[name]
            nc.sync.dma_start(s.ap[:, 0:f], weights[name][o[i]:o[i + 1]].rearrange("(p f) -> p f", p=P))\
                .then_inc(raw_sem[k], 16)
            return s, (raw_sem[k], 16 * turn, f"w{k}")

        plan = split_plan()
        ready = []
        planned = [0]

        def split_next():
            name, i = plan[planned[0]]
            planned[0] += 1
            r, tl = load(name, i)
            f = CHUNKS[name][i]
            s = pairs.take()
            SC.wait(tl, s.free)
            t1 = SC.done(sc.activation(s.ap.hi[:, 0:f], r.ap[:, 0:f], ACT.Copy))
            VE.wait(t1, tl, s.free)
            t2 = VE.done(ve.tensor_tensor(s.ap.lo[:, 0:f], r.ap[:, 0:f], s.ap.hi[:, 0:f].bitcast(F32), ALU.subtract))
            r.free = [t2]
            ready.append((name, i, s, t2))

        def load_pair(name, i):
            while len(ready) < 2 and planned[0] < len(plan):
                split_next()
            n, j, s, t = ready.pop(0)
            assert (n, j) == (name, i), (n, j, name, i)
            return s, t

        nload = [0]

        def fetch(dst, src, *tokens):
            s = sem(f"s_l{nload[0]}")
            nload[0] += 1
            SC.wait(*tokens)
            sc.dma_start(dst, src).then_inc(s, 16)
            return (s, 16, f"l{nload[0]}")

        def vec(name, i=0):
            o, _ = VEC_AT[name]
            return VEC[:, o + i:o + i + 1]

        def const(name):
            o, n = CONST_AT[name]
            return consts[:, o:o + n]

        ident = CONST[:, 0:128]
        ones = CONST[:, 128:256]
        bones = CONST[:, 256:384]
        t_const = fetch(CONST[:, :], consts[:, 0:384])
        t_vec = fetch(VEC[:, :], vecs)
        t_x = fetch(X[:, :, :], xT.rearrange("(k p) t -> p k t", p=P))
        t_xc = fetch(XC[:, :, :], ctxT.rearrange("(k p) t -> p k t", p=P))
        for e in (PE, VE, SC, GP):
            e.wait(t_const, t_vec)

        state = {"x": [t_x] * KT, "xc": [t_xc] * KT, "arena_free": []}

        def mm_group(out, pairs_, deps):
            PE.wait(*deps)
            n = len(pairs_)
            for i, (l, r) in enumerate(pairs_):
                ins = pe.matmul(out, l, r, start=(i == 0), stop=(i == n - 1))
            return PE.done(ins)

        def mm_pair(out, operands, first, final):
            n = len(operands)
            for i, (l, r) in enumerate(operands):
                pe.matmul(out, l.hi, r.hi, start=(first and i == 0), stop=False)
                pe.matmul(out, l.hi, r.lo, start=False, stop=False)
                ins = pe.matmul(out, l.lo, r.hi, start=False, stop=(final and i == n - 1))
            return ins

        SC.done(sc.activation(CS[:, :, 0], VEC[:, 0:8], ACT.Silu))
        t_cs = SC.done(sc.activation(CS[:, :, 1], VEC[:, 8:16], ACT.Silu))
        t_mod = {}

        ada_rows = []

        def ada_end():
            layer, c, rows, t_rows = ada_rows.pop()
            b = bank()
            PE.wait(t_rows, b.free)
            for q in range(4):
                ins = pe.matmul(b.ap[:, 2 * q:2 * q + 2], rows[0:2, 128 * q:128 * q + 128], ident[0:2, 0:2],
                                start=True, stop=True)
            t = PE.done(ins)
            VE.wait(t)
            o = VEC_AT["ada_b"][0] + 48 * layer + 4 * c
            t = VE.done(ve.tensor_tensor(MOD[:, layer, 4 * c:4 * c + 4, :],
                                         b.ap[:, 0:8].rearrange("p (m c) -> p m c", m=4),
                                         VEC[:, o:o + 4].unsqueeze(2).broadcast_to([P, 4, 2]), ALU.add))
            b.free = [t]
            row_read[0] = t
            part = c // 2
            t_mod[(layer, part)] = t
            if c % 2 and part in (1, 4):
                which = 0 if part == 1 else 1
                g = VEC_AT[("norm1_g", "norm2_g")[which]][0] + 8 * layer
                VE.wait(t)
                for cond in range(2):
                    t = VE.done(ve.scalar_tensor_tensor(
                        out=GS[:, layer, which, :, cond], in0=MOD[:, layer, 8 * part:8 * part + 8, cond], scalar=1.0,
                        in1=VEC[:, g:g + 8], op0=ALU.add, op1=ALU.mult))
                t_mod[(layer, part)] = t

        row_read = [None]

        def ada_chunk(layer, i, arrived=None):
            if ada_rows:
                ada_end()
            s, tl = arrived or load(f"ada{layer}", i)
            c, q = divmod(i, 4)
            b = banks[7]
            w = s.ap.rearrange("p (k n) -> p k n", k=2)
            PE.wait(tl, t_cs, b.free)
            for k in range(2):
                ins = pe.matmul(b.ap[0:2, :], CS[:, 2 * q + k, :], w[:, k, :], start=(q == 0 and k == 0),
                                stop=(q == 3 and k == 1))
            t = PE.done(ins)
            s.free = [t]
            if q == 3:
                SC.wait(t, row_read[0])
                t = SC.done(sc.activation(ROWS[0:2, :], b.ap[0:2, :], ACT.Copy))
                b.free = [t]
                ada_rows.append((layer, c, ROWS, t))

        def mod(layer, part, m, c):
            return MOD[:, layer, part * 8 + m, c:c + 1]

        side = []

        ada_on_way = []

        def ada_load():
            layer, i = side.pop(0)
            k = ada_ring.i % 2
            turn = ada_ring.i // 2 + 1
            s = ada_ring.take()
            sp_wait(s.free)
            o = offsets[f"ada{layer}"]
            nc.sync.dma_start(s.ap, weights[f"ada{layer}"][o[i]:o[i + 1]].rearrange("(p f) -> p f", p=P))\
                .then_inc(ada_sem[k], 16)
            ada_on_way.append((layer, i, (s, (ada_sem[k], 16 * turn, f"a{k}"))))

        def run_side(n=1):
            for _ in range(n):
                if ada_on_way:
                    ada_chunk(*ada_on_way.pop(0))
                elif ada_rows:
                    ada_end()
                while side and len(ada_on_way) < 2:
                    ada_load()

        t_eps = [VE.done(ve.memset(SM[:, 0:1], EPS)), VE.done(ve.memset(SM[:, 1:2], SUB_EPS))]
        SC.wait(t_eps)

        def eps_ap(eps):
            return SM[:, 0:1] if eps == EPS else SM[:, 1:2]

        def rstd_of(b, rows, n, count, eps, out, tb, deps=()):
            s = tmp.take()
            SC.wait(tb, s.free)
            t = SC.done(sc.activation(s.ap[rows, 0:n], b.ap[rows, 0:n], ACT.Sqrt, bias=eps_ap(eps)[rows, :],
                                      scale=1.0 / count))
            b.free = [t]
            VE.wait(t, *deps)
            t = VE.done(ve.reciprocal(out, s.ap[rows, 0:n]))
            s.free = [t]
            return t

        rs_free = {}

        def norm_rstd(src, n, tok, nk, count, rs_off):
            b = bank()
            tb = None
            for k in range(nk):
                s = tmp.take()
                SC.wait(tok[k], s.free)
                ts = SC.done(sc.activation(s.ap[:, 0:n], src[:, k, :], ACT.Square))
                PE.wait(ts, b.free)
                tb = PE.done(pe.matmul(b.ap[:, 0:n], ones, s.ap[:, 0:n], start=(k == 0), stop=(k == nk - 1)))
                s.free = [tb]
            return rstd_of(b, slice(0, P), n, count, EPS, RS[:, rs_off:rs_off + n], tb, [rs_free.get(rs_off)])

        def norm(src, dst, n, tok, nk, count, gain, rs_off):
            tr = norm_rstd(src, n, tok, nk, count, rs_off)
            out = []
            VE.wait(tr)
            for k in range(nk):
                VE.wait(tok[k])
                out.append(VE.done(ve.scalar_tensor_tensor(out=dst[:, k, :], in0=src[:, k, :], scalar=gain(k),
                                                           in1=RS[:, rs_off:rs_off + n], op0=ALU.mult, op1=ALU.mult)))
            rs_free[rs_off] = out[-1]
            return out

        def norm_pair(src, dst, n, tok, tr, gain, shift, rs_off):
            out = []

            def rounded(k, v, s, t_hi):
                lo, hi = dst.lo[:, k, :], dst.hi[:, k, :].bitcast(F32)
                VE.wait(t_hi)
                if shift is None:
                    t_lo = VE.done(ve.tensor_tensor(lo, v, hi, ALU.subtract))
                else:
                    t_lo = VE.done(ve.scalar_tensor_tensor(out=lo, in0=v, scalar=shift(k), in1=hi,
                                                           op0=ALU.add, op1=ALU.subtract))
                s.free = [t_lo]
                out.append(t_lo)

            VE.wait(tr)
            before = None
            for k in range(KT):
                s = tmp.take()
                v = s.ap[:, 0:n]
                VE.wait(tok[k], s.free)
                t_v = VE.done(ve.scalar_tensor_tensor(out=v, in0=src[:, k, :], scalar=gain(k),
                                                      in1=RS[:, rs_off:rs_off + n], op0=ALU.mult, op1=ALU.mult))
                SC.wait(t_v)
                if shift is None:
                    t_hi = SC.done(sc.activation(dst.hi[:, k, :], v, ACT.Copy))
                else:
                    t_hi = SC.done(sc.activation(dst.hi[:, k, :], v, ACT.Identity, bias=shift(k)))
                if before:
                    rounded(*before)
                before = (k, v, s, t_hi)
            rs_free[rs_off] = t_v
            rounded(*before)
            return out

        def norm_main(H, HC, gain_of, shift_of, deps):
            if HC is not None:
                tc = norm_rstd(XC, NC, state["xc"], KT, D, NL)
            tr = norm_rstd(X, NL, state["x"], KT, D, 0)
            VE.wait(state["arena_free"], *deps)
            SC.wait(state["arena_free"], *deps)
            r = [norm_pair(X, H, NL, state["x"], tr, gain_of(0), shift_of and shift_of(0), 0)]
            if HC is not None:
                r.append(norm_pair(XC, HC, NC, state["xc"], tc, gain_of(1), shift_of and shift_of(1), NL))
            return r

        def second_gain(name, first=0):
            return lambda c: (lambda k: vec(name, first + k))

        def columns(s, k=8):
            return Pair(s.ap.hi[:, 0:128 * k].rearrange("p (k n) -> p k n", k=k),
                        s.ap.lo[:, 0:128 * k].rearrange("p (k n) -> p k n", k=k))

        def residual(m, seg, b, tb, scale):
            x, key = ((X, "x"), (XC, "xc"))[seg]
            VE.wait(tb, state[key][m])
            t = VE.done(ve.scalar_tensor_tensor(out=x[:, m, :], in0=b.ap[:, 0:x.shape[2]], scalar=scale,
                                                in1=x[:, m, :], op0=ALU.mult, op1=ALU.add))
            b.free = [t]
            state[key][m] = t

        def ffn(up, down, segs, th, conv, scale, scale_dep):
            at = 0
            for g, (k0, k1) in enumerate(GROUPS):
                for j in range(at, min(k1 + 1, FT)):
                    run_side(2)
                    sg, tlg = load_pair(up, 2 * j)
                    sv, tlv = load_pair(up, 2 * j + 1)
                    wg, wv = columns(sg), columns(sv)
                    gates = []
                    PE.wait(tlg)
                    for si, (h, _, n) in enumerate(segs):
                        bg = bank()
                        PE.wait(bg.free)
                        for k in range(KT):
                            PE.wait(th[si][k])
                            ins = mm_pair(bg.ap[:, 0:n], [(wg[:, k, :], h[:, k, :])], k == 0, k == KT - 1)
                        tg = PE.done(ins)
                        gates.append((bg, tg))
                    sg.free = [tg]
                    PE.wait(tlv)
                    for si, (h, hid, n) in enumerate(segs):
                        bg, tg = gates[si]
                        bv = bank()
                        PE.wait(bv.free)
                        tv = PE.done(mm_pair(bv.ap[:, 0:n], [(wv[:, k, :], h[:, k, :]) for k in range(8)], True, True))
                        a = tmp.take()
                        av, gv = a.ap[:, 0:n], bg.ap[:, 0:n]
                        if conv is None:
                            SC.wait(tg, a.free)
                            t = SC.done(sc.activation(av, gv, ACT.Silu))
                            bg.free = [t]
                        else:
                            o = VEC_AT["ffn_conv_w"][0] + 66 * conv + j
                            ob = VEC_AT["ffn_conv_b"][0] + 22 * conv + j
                            SC.wait(tg, a.free)
                            t = SC.done(sc.activation(av, gv, ACT.Identity, bias=VEC[:, ob:ob + 1],
                                                      scale=VEC[:, o + 22:o + 23]))
                            VE.wait(t)
                            t = VE.done(ve.scalar_tensor_tensor(out=av[:, 1:n], in0=gv[:, 0:n - 1], scalar=VEC[:, o:o + 1],
                                                                in1=av[:, 1:n], op0=ALU.mult, op1=ALU.add))
                            VE.wait(t)
                            t = VE.done(ve.scalar_tensor_tensor(out=av[:, 0:n - 1], in0=gv[:, 1:n],
                                                                scalar=VEC[:, o + 44:o + 45],
                                                                in1=av[:, 0:n - 1], op0=ALU.mult, op1=ALU.add))
                            bg.free = [t]
                            SC.wait(t)
                            t = SC.done(sc.activation(av, av, ACT.Silu))
                        VE.wait(t, tv)
                        t = VE.done(ve.tensor_tensor(av, bv.ap[:, 0:n], av, ALU.mult))
                        bv.free = [t]
                        hi, lo = hid.hi[:, j % HID, :], hid.lo[:, j % HID, :]
                        SC.wait(t)
                        t = SC.done(sc.activation(hi, av, ACT.Copy))
                        VE.wait(t)
                        t_hid = VE.done(ve.tensor_tensor(lo, av, hi.bitcast(F32), ALU.subtract))
                        a.free = [t_hid]
                    sv.free = [tv]
                    if j == k1 - 1:
                        t_full = t_hid
                at = min(k1 + 1, FT)
                for m in range(8):
                    s, tl = load_pair(down, 8 * g + m)
                    w = columns(s, k1 - k0)
                    PE.wait(tl, t_full)
                    for si, (_, hid, n) in enumerate(segs):
                        b = bank()
                        PE.wait(b.free)
                        t = PE.done(mm_pair(b.ap[:, 0:n], [(w[:, k - k0, :], hid[:, k % HID, :])
                                                           for k in range(k0, k1)], True, True))
                        VE.wait(scale_dep)
                        residual(m, si, b, t, scale(m, si))
                    s.free = [t]
            return t

        def modulated_ffn(up, down, layer, with_ctx):
            with ExitStack() as scope:
                segs = [(alloc_pair(scope, KT, NL), alloc_pair(scope, HID, NL), NL)]
                if with_ctx:
                    segs.append((alloc_pair(scope, KT, NC), alloc_pair(scope, HID, NC), NC))
                t_scale, t_shift = t_mod[(layer, 4)], t_mod[(layer, 3)]
                th = norm_main(segs[0][0], segs[1][0] if with_ctx else None,
                               lambda c: (lambda k: GS[:, layer, 1, k, c:c + 1]),
                               lambda c: (lambda k: mod(layer, 3, k, c)), [t_scale, t_shift])
                state["arena_free"] = [ffn(up, down, segs, th, layer, lambda m, si: mod(layer, 5, m, si),
                                           t_mod[(layer, 5)])]

        def half_ffn(up, down, gain):
            with ExitStack() as scope:
                segs = [(alloc_pair(scope, KT, NL), alloc_pair(scope, HID, NL), NL)]
                th = norm_main(segs[0][0], None, gain, None, [])
                state["arena_free"] = [ffn(up, down, segs, th, None, lambda m, si: 0.5, None)]

        def project_out(name, mixes, tok, scale, scale_dep):
            for m in range(8):
                s, tl = load_pair(name, m)
                w = columns(s)
                PE.wait(tl)
                for si, mix in enumerate(mixes):
                    n = (NL, NC)[si]
                    b = bank()
                    PE.wait(b.free)
                    for k in range(KT):
                        PE.wait(tok[KT * si + k])
                        ins = mm_pair(b.ap[:, 0:n], [(w[:, k, :], mix[:, k, :])], k == 0, k == KT - 1)
                    t = PE.done(ins)
                    VE.wait(scale_dep)
                    residual(m, si, b, t, scale(m, si))
                s.free = [t]
            return t

        heads = []

        def advance():
            for head in list(heads):
                if next(head, "end") == "end":
                    heads.remove(head)

        def project(name, i, streams, use):
            s, tl = load_pair(name, i)
            w = columns(s)
            for si, (h, n, th) in enumerate(streams):
                b = bank()
                PE.wait(tl, b.free)
                for k in range(KT):
                    PE.wait(th[k])
                    ins = mm_pair(b.ap[:, 0:n], [(w[:, k, :], h[:, k, :])], k == 0, k == KT - 1)
                t = PE.done(ins)
                s.free = [t]
                advance()
                head = use(si, b, t)
                if head:
                    heads.append(head)
                    next(head)

        def token_rows(name, halves, blocks, use):
            for c in range(halves):
                bs = [bank() for _ in blocks]
                for q in range(4):
                    s, tl = load_pair(name, 4 * c + q)
                    w = Pair(s.ap.hi.rearrange("p (k n) -> p k n", k=2), s.ap.lo.rearrange("p (k n) -> p k n", k=2))
                    PE.wait(tl)
                    for bi, (b, h) in enumerate(zip(bs, blocks)):
                        PE.wait(b.free)
                        ins = mm_pair(b.ap, [(h(2 * q + k), w[:, k, :]) for k in range(2)], q == 0, q == 3)
                        if q == 3:
                            t = PE.done(ins)
                            use(c, bi, b, t)
                            s.free = [t]
                    if q < 3:
                        s.free = [PE.done(ins)]
                    advance()

        def run_units(units):
            n = len(units)
            for i in range(n + 3):
                if i < n:
                    units[i]["scores"]()
                if 0 <= i - 2 < n:
                    units[i - 2]["turn"]()
                if i < n:
                    units[i]["weights"]()
                if 0 <= i - 3 < n:
                    units[i - 3]["values"]()

        score_banks = Rotor([(banks[0], banks[1]), (banks[2], banks[3])])
        turn_banks = Rotor([(banks[4], banks[5])])
        value_banks = Rotor([banks[6], banks[7]])
        small = Rotor([Slot(MN[:, i, :]) for i in range(8)])

        def turn(p, blocks, tp, prot):
            ba, bb = turn_banks.take()
            PE.wait(tp, ba.free, bb.free if len(blocks) > 3 else None)
            for i, c in enumerate(blocks):
                b = ba if i < 3 else bb
                ins = pe.transpose(b.ap[:, (i % 3) * 128:(i % 3) * 128 + 128], p.ap[:, c * 128:(c + 1) * 128], ident)
            t = PE.done(ins)
            p.free = [t]
            o = prot.take()
            n1 = min(len(blocks), 3) * 128
            n2 = (len(blocks) - 3) * 128
            SC.wait(t, o.free)
            t1 = SC.done(sc.activation(o.ap[:, 0:n1], ba.ap[:, 0:n1], ACT.Copy))
            ba.free = [t1]
            if n2 <= 0:
                return o, t1
            VE.wait(t, o.free)
            t2 = VE.done(ve.tensor_copy(o.ap[:, 384:384 + n2], bb.ap[:, 0:n2]))
            bb.free = [t2]
            return o, [t1, t2]

        def softmax_unit(q, k, nk, scale, causal, v, deps, t_v, prot, trot, finish):
            u = {}

            def scores():
                sb_ = score_banks.take()
                u["b"] = sb_
                PE.wait(deps, sb_[0].free)
                if nk <= 512:
                    u["t"] = PE.done(pe.matmul(sb_[0].ap[:, 0:nk], q, k[:, 0:nk], start=True, stop=True))
                else:
                    PE.wait(sb_[1].free)
                    half = nk // 2
                    pe.matmul(sb_[0].ap[:, 0:half], q, k[:, 0:half], start=True, stop=True)
                    u["t"] = PE.done(pe.matmul(sb_[1].ap[:, 0:half], q, k[:, half:nk], start=True, stop=True))

            def weights_():
                b0, b1 = u["b"]
                i0 = banks.index(b0)
                m = small.take()
                p = prot.take()
                u["m"], u["p"] = m, p
                VE.wait(u["t"], m.free)
                SC.wait(p.free)
                if causal:
                    ve.tensor_reduce(m.ap[0:64, 0:1], b0.ap[0:64, 0:nk - 64], AX.X, ALU.max)
                    t = VE.done(ve.tensor_reduce(m.ap[64:128, 0:1], b0.ap[64:128, 0:nk], AX.X, ALU.max))
                elif nk <= 512:
                    t = VE.done(ve.tensor_reduce(m.ap[:, 0:1], b0.ap[:, 0:nk], AX.X, ALU.max))
                else:
                    t = VE.done(ve.tensor_reduce(m.ap[:, 0:1], ps[:, i0:i0 + 2, 0:nk // 2], AX.XY, ALU.max))
                VE.wait(t)
                t = VE.done(ve.tensor_scalar(m.ap[:, 1:2], m.ap[:, 0:1], -scale, None, ALU.mult))
                SC.wait(t)
                if causal:
                    GP.wait(p.free)
                    tz = GP.done(gp.memset(p.ap[0:64, nk - 64:nk], 0.0))
                    sc.activation(p.ap[0:64, 0:nk - 64], b0.ap[0:64, 0:nk - 64], ACT.Exp, bias=m.ap[0:64, 1:2],
                                  scale=scale, accum_out=m.ap[0:64, 2:3])
                    t = SC.done(sc.activation(p.ap[64:128, 0:nk], b0.ap[64:128, 0:nk], ACT.Exp,
                                              bias=m.ap[64:128, 1:2], scale=scale, accum_out=m.ap[64:128, 2:3]))
                    b0.free = [t]
                    t = [t, tz]
                elif nk <= 512:
                    t = SC.done(sc.activation(p.ap[:, 0:nk], b0.ap[:, 0:nk], ACT.Exp, bias=m.ap[:, 1:2], scale=scale,
                                              accum_out=m.ap[:, 2:3]))
                    b0.free = [t]
                else:
                    t = SC.done(sc.activation(p.ap[:, 0:nk].rearrange("p (a n) -> p a n", a=2),
                                              ps[:, i0:i0 + 2, 0:nk // 2], ACT.Exp, bias=m.ap[:, 1:2], scale=scale,
                                              accum_out=m.ap[:, 2:3]))
                    b0.free = [t]
                    b1.free = [t]
                u["tp"] = t

            def turn_():
                u["o"], u["to"] = turn(u["p"], list(range(nk // 128)), u["tp"], trot)
                m = u["m"]
                VE.wait(u["tp"])
                u["tr"] = VE.done(ve.reciprocal(m.ap[:, 3:4], m.ap[:, 2:3]))

            def values():
                b = value_banks.take()
                n = nk // 128
                PE.wait(u["to"], b.free, t_v)
                for kb in range(n):
                    vv = v(kb)
                    ins = pe.matmul(b.ap[:, 0:vv.shape[1]], u["o"].ap[:, kb * 128:(kb + 1) * 128], vv,
                                    start=(kb == 0), stop=(kb == n - 1))
                t = PE.done(ins)
                u["o"].free = [t]
                VE.wait(t, u["tr"])
                finish(b, u["m"].ap, u["m"])

            return dict(scores=scores, weights=weights_, turn=turn_, values=values)

        def turn_mix(src, blocks, dst, toks, use=None):
            out = []
            for k in range(8):
                b = bank()
                PE.wait(toks, b.free)
                for i, tb in enumerate(blocks):
                    ins = pe.transpose(b.ap[:, i * 128:(i + 1) * 128], src(tb)[:, k * 128:(k + 1) * 128], ident)
                t = PE.done(ins)
                n = 128 * len(blocks)
                out.append(use(k, b, n, t) if use else pair_from(b, b.ap[:, 0:n], dst.hi[:, k, :], dst.lo[:, k, :], t))
            return out

        def pair_from(slot, v, hi, lo, t, t_free=None):
            SC.wait(t, t_free)
            t1 = SC.done(sc.activation(hi, v, ACT.Copy))
            VE.wait(t, t1, t_free)
            t2 = VE.done(ve.tensor_tensor(lo, v, hi.bitcast(F32), ALU.subtract))
            slot.free = [t2]
            return t2

        def even_mixer():
            layer = 0
            with ExitStack() as base:
                MT = alloc(base, 6, 1024)
                CP = alloc(base, 3840)
                GR = alloc(base, 4, NT)
                KG = alloc(base, 2, NT)
                VG = alloc(base, 6, 128)
                ROT = alloc(base, 256)
                C = CP[:, :].rearrange("p (h t) -> p h t", h=5)
                ro = CONST_AT["rot_g"][0]
                t_ro = fetch(ROT[:, :], consts[:, ro:ro + 256])
                rot_g = ROT[:, 0:128]
                rot_m = ROT[:, 128:256]
                KR = MT[:, 1, 0:NT]
                RM = MT[:, 0, :]
                t_c, t_g = [], []
                spans = ((NC, NL), (0, NC))
                with ExitStack() as scope:
                    H = alloc_pair(scope, KT, NL)
                    HC = alloc_pair(scope, KT, NC)
                    RG = alloc(scope, 1024)
                    t_rg = fetch(RG[:, :], const("rope_g"))
                    th = norm_main(H, HC, lambda c: (lambda k: GS[:, layer, 0, k, c:c + 1]),
                                   lambda c: (lambda k: mod(layer, 0, k, c)), [t_mod[(0, 0)], t_mod[(0, 1)]])
                    streams = [(H, NL, th[0]), (HC, NC, th[1])]

                    def keep(dst, rows=slice(0, P)):
                        toks = [None, None]

                        def use(si, b, t):
                            off, n = spans[si]
                            SC.wait(t)
                            t = SC.done(sc.activation(dst[rows, off:off + n], b.ap[rows, 0:n], ACT.Copy))
                            b.free = [t]
                            toks[si] = t
                        return use, toks

                    for i in range(5):
                        use, toks = keep(C[:, i, :])
                        project("att_in", i, streams, use)
                        run_side(3)
                        t_c.append(toks)
                    use, t_kr = keep(KR, slice(64, 96))
                    project("att_in", 5, streams, use)

                    def pair_heads(i, g, dsts):
                        def use(si, b, tb):
                            off, n = spans[si]
                            s = tmp.take()
                            SC.wait(tb, s.free)
                            t = SC.done(sc.activation(s.ap[:, 0:n], b.ap[:, 0:n], ACT.Square))
                            yield
                            b2 = bank()
                            tq = mm_group(b2.ap[:, 0:n], [(bones, s.ap[:, 0:n])], [t, b2.free])
                            s.free = [tq]
                            r = tmp.take()
                            VE.wait(r.free)
                            t = rstd_of(b2, slice(0, P), n, 64, EPS, r.ap[:, 0:n], tq)
                            VE.wait(t)
                            if si == 1:
                                for rows, dst in dsts:
                                    t = VE.done(ve.scalar_tensor_tensor(
                                        out=dst(off, n), in0=b.ap[rows, 0:n], scalar=VEC[rows, g:g + 1],
                                        in1=r.ap[rows, 0:n], op0=ALU.mult, op1=ALU.mult))
                                r.free = [t]
                                b.free = [t]
                                t_g[i][1] = t
                                return
                            q = tmp.take()
                            VE.wait(q.free)
                            t = VE.done(ve.scalar_tensor_tensor(out=q.ap, in0=b.ap, scalar=VEC[:, g:g + 1], in1=r.ap,
                                                                op0=ALU.mult, op1=ALU.mult))
                            r.free = [t]
                            b.free = [t]
                            yield
                            b3 = bank()
                            tr = mm_group(b3.ap, [(rot_g, q.ap)], [t, t_ro, b3.free])
                            u = tmp.take()
                            VE.wait(tr, u.free, t_rg)
                            t1 = VE.done(ve.tensor_tensor(u.ap, b3.ap, RG[:, 512:1024], ALU.mult))
                            b3.free = [t1]
                            t2 = VE.done(ve.tensor_tensor(q.ap, q.ap, RG[:, 0:512], ALU.mult))
                            VE.wait(t1, t2)
                            for rows, dst in dsts:
                                t = VE.done(ve.tensor_tensor(dst(off, n), q.ap[rows, :], u.ap[rows, :], ALU.add))
                            q.free = [t]
                            u.free = [t]
                            t_g[i][0] = t
                        return use

                    whole = slice(0, P)
                    for i in range(4):
                        t_g.append([None, None])
                        project("att_in", 6 + i, streams,
                                pair_heads(i, VEC_AT["gqa_q_g"][0],
                                           [(whole, lambda off, n, i=i: GR[:, i, off:off + n])]))
                        run_side(2)
                    t_g.append([None, None])
                    lo_, hi_ = slice(0, 64), slice(64, 128)
                    project("att_in", 10, streams,
                            pair_heads(4, VEC_AT["gqa_k_g"][0],
                                       [(lo_, lambda off, n: KG[0:64, 0, off:off + n]),
                                        (lo_, lambda off, n: KG[64:128, 0, off:off + n]),
                                        (hi_, lambda off, n: KG[0:64, 1, off:off + n]),
                                        (hi_, lambda off, n: KG[64:128, 1, off:off + n])]))
                    s, tl = load_pair("att_in", 11)
                    w = columns(s)
                    for tb in range(6):
                        src, c = (HC, tb) if tb < 2 else (H, tb - 2)
                        b = bank()
                        PE.wait(tl, b.free)
                        t = PE.done(mm_pair(b.ap[:, 0:128],
                                            [(src[:, k, c * 128:(c + 1) * 128], w[:, k, :]) for k in range(8)],
                                            True, True))
                        s.free = [t]
                        SC.wait(t)
                        t_vg = SC.done(sc.activation(VG[:, tb, :], b.ap[:, 0:128], ACT.Copy))
                        t_last_h = t
                        b.free = [t_vg]
                        advance()

                    while heads:
                        advance()

                t_cn = [[None] * 2 for _ in range(5)]
                for a0, a1, name in ((0, 3, "mla_qa_g"), (3, 5, "mla_kva_g")):
                    for si, (off, n) in enumerate(spans):
                        v = C[:, a0:a1, off:off + n]
                        r = norm(v, v, n, [t_c[k][si] for k in range(a0, a1)], a1 - a0, 128 * (a1 - a0),
                                 lambda k: vec(name, k), NL * si)
                        for k in range(a0, a1):
                            t_cn[k][si] = r[k - a0]

                with ExitStack() as scope:
                    QL = alloc(scope, 8, NL)
                    QC = alloc(scope, 8, NC)
                    K = alloc(scope, 8, NT)
                    V = alloc(scope, 6, 512)
                    free = [t_last_h, t_g[4][0]]
                    t_rm = fetch(RM, const("rope_m"), free)
                    VE.wait(free)

                    def mla_head(src, tb, n, dst, g, rope, on_free, put):
                        s = tmp.take()
                        SC.wait(tb, s.free)
                        t = SC.done(sc.activation(s.ap[0:96, 0:n], src, ACT.Square))
                        yield
                        b2 = bank()
                        tq = mm_group(b2.ap[0:96, 0:n], [(ones[0:96, 0:96], s.ap[0:96, 0:n])], [t, b2.free])
                        s.free = [tq]
                        r = tmp.take()
                        VE.wait(r.free)
                        t = rstd_of(b2, slice(0, 96), n, 96, EPS, r.ap[0:96, 0:n], tq)
                        VE.wait(t, tb)
                        t = VE.done(ve.scalar_tensor_tensor(out=dst, in0=src, scalar=VEC[0:96, g:g + 1],
                                                            in1=r.ap[0:96, 0:n], op0=ALU.mult, op1=ALU.mult))
                        r.free = [t]
                        on_free(t)
                        if not rope:
                            put(t)
                            return
                        yield
                        b3 = bank()
                        tr = mm_group(b3.ap[64:96, 0:n], [(rot_m[64:96, 64:96], dst[64:96, :])], [t, t_ro, b3.free])
                        u = tmp.take()
                        VE.wait(tr, u.free, t_rm)
                        t1 = VE.done(ve.tensor_tensor(u.ap[64:96, 0:n], b3.ap[64:96, 0:n], RM[64:96, 512:1024],
                                                      ALU.mult))
                        b3.free = [t1]
                        t2 = VE.done(ve.tensor_tensor(dst[64:96, :], dst[64:96, :], RM[64:96, 0:512], ALU.mult))
                        VE.wait(t1, t2)
                        t = VE.done(ve.tensor_tensor(dst[64:96, :], dst[64:96, :], u.ap[64:96, 0:n], ALU.add))
                        u.free = [t]
                        put(t)

                    t_q = [[None] * 2 for _ in range(8)]
                    t_k = [[None] * 2 for _ in range(8)]
                    gq = VEC_AT["mla_q_g"][0]
                    gk = VEC_AT["mla_k_g"][0]
                    s, tl = load("kb", 0)
                    w = s.ap[:, 0:1024].rearrange("p (h k n) -> p h k n", h=8, k=2)
                    SC.wait(free)
                    for h in range(8):
                        run_side(1)
                        for si, (off, n) in enumerate(spans):
                            b = bank()
                            tb = mm_group(b.ap[0:64, 0:n], [(w[:, h, k, :], C[:, 3 + k, off:off + n]) for k in range(2)],
                                          [tl, b.free, [t_cn[3 + k][si] for k in range(2)]])
                            s.free = [tb]
                            GP.wait(t_kr, free)
                            tg = GP.done(gp.tensor_copy(K[64:96, h, off:off + n], KR[64:96, off:off + n]))
                            SC.wait(tb)
                            t = SC.done(sc.activation(K[0:64, h, off:off + n], b.ap[0:64, 0:n], ACT.Copy))
                            b.free = [t]
                            dst = K[0:96, h, off:off + n]
                            advance()
                            heads.append(mla_head(dst, [t, tg], n, dst, gk, si == 0, lambda t: None,
                                                  lambda t, h=h, si=si: t_k[h].__setitem__(si, t)))
                            next(heads[-1])
                    for c in range(4):
                        s, tl = load("qb", c)
                        w = s.ap[:, 0:576].rearrange("p (h k n) -> p h k n", h=2, k=3)
                        for h2 in range(2):
                            h = 2 * c + h2
                            run_side(1)
                            for si, (off, n) in enumerate(spans):
                                b = bank()
                                tb = mm_group(b.ap[0:96, 0:n],
                                              [(w[:, h2, k, :], C[:, k, off:off + n]) for k in range(3)],
                                              [tl, b.free, [t_cn[k][si] for k in range(3)]])
                                s.free = [tb]

                                def on_free(t, b=b):
                                    b.free = [t]

                                advance()
                                heads.append(mla_head(b.ap[0:96, 0:n], tb, n, (QL, QC)[si][0:96, h, :], gq, si == 0,
                                                      on_free, lambda t, h=h, si=si: t_q[h].__setitem__(si, t)))
                                next(heads[-1])
                    s, tl = load("vb", 0)
                    w = s.ap[:, 0:1024].rearrange("p (k n) -> p k n", k=2)
                    for tb in range(6):
                        b = bank()
                        t = mm_group(b.ap, [(C[:, 3 + k, tb * 128:(tb + 1) * 128], w[:, k, :]) for k in range(2)],
                                     [tl, b.free])
                        s.free = [t]
                        t_clast = t
                        SC.wait(t)
                        t_v = SC.done(sc.activation(V[:, tb, :], b.ap, ACT.Copy))
                        b.free = [t_v]
                        advance()
                    while heads:
                        advance()

                    prot = Rotor([Slot(CP[:, 768 * i:768 * i + 768]) for i in range(2)])
                    trot = Rotor([Slot(CP[:, 1536 + 768 * i:2304 + 768 * i]) for i in range(3)])
                    for s in prot.slots + trot.slots:
                        s.free = [t_clast]
                    t_mix = []

                    def finish_in(dst):
                        def finish(b, m, slot):
                            t = VE.done(ve.tensor_scalar(dst, b.ap[:, 0:64], m[:, 3:4], None, ALU.mult))
                            b.free = [t]
                            slot.free = [t]
                            t_mix.append(t)
                        return finish

                    units = []
                    for h in range(8):
                        for si, nk in ((0, NT), (1, NC)):
                            for qb in range((4, 2)[si]):
                                q = (QL, QC)[si][0:96, h, qb * 128:(qb + 1) * 128]
                                tb = qb + (2 if si == 0 else 0)
                                units.append(softmax_unit(
                                    q, K[0:96, h, 0:nk], nk, 96.0 ** -0.5, False,
                                    lambda kb, h=h: V[:, kb, 64 * h:64 * h + 64], [t_q[h][si], t_k[h]], t_v,
                                    prot, trot, finish_in(MT[:, tb, 64 * h:64 * h + 64])))
                    for h in range(8):
                        rows = slice(64 * (h % 2), 64 * (h % 2) + 64)
                        g = h // 4
                        for si, nk in ((0, NT), (1, NC)):
                            for qb in range((4, 2)[si]):
                                tb = qb + (2 if si == 0 else 0)
                                units.append(softmax_unit(
                                    GR[rows, h // 2, tb * 128:(tb + 1) * 128], KG[rows, g, 0:nk], nk, 0.125, False,
                                    lambda kb, g=g: VG[:, kb, 64 * g:64 * g + 64], [t_g[h // 2], t_g[4]], t_vg,
                                    prot, trot, finish_in(MT[:, tb, 512 + 64 * h:576 + 64 * h])))
                    run_side(99)
                    run_units(units)

                with ExitStack() as scope:
                    M = alloc_pair(scope, KT, NL)
                    MC = alloc_pair(scope, KT, NC)
                    t = turn_mix(lambda tb: MT[:, tb, :], [2, 3, 4, 5], M, t_mix)
                    t += turn_mix(lambda tb: MT[:, tb, :], [0, 1], MC, t_mix)
                    t_end = project_out("att_out", [M, MC], t, lambda m, si: mod(0, 2, m, si), t_mod[(0, 2)])
                    state["arena_free"] = [t_end]

        def odd_mixer():
            layer = 1
            with ExitStack() as base:
                KK = alloc(base, 4, NT)
                QQ = alloc(base, 4, NL)
                V = alloc(base, 6, 1024)
                O = alloc(base, 8, NL)
                G = alloc(base, NT)
                F = alloc(base, NT)
                M = alloc(base, NL)
                COL = alloc(base, 2, 2, 4, 8)
                with ExitStack() as scope:
                    H = alloc_pair(scope, KT, NL)
                    HC = alloc_pair(scope, KT, NC)
                    GATE = alloc(scope, NT)
                    th = norm_main(H, HC, lambda c: (lambda k: GS[:, layer, 0, k, c:c + 1]),
                                   lambda c: (lambda k: mod(layer, 0, k, c)), [t_mod[(1, 0)], t_mod[(1, 1)]])
                    streams = [(H, NL, th[0]), (HC, NC, th[1])]
                    spans = ((NC, NL), (0, NC))
                    t_gate = []

                    def gate(si, b, t):
                        off, n = spans[si]
                        SC.wait(t)
                        t = SC.done(sc.activation(GATE[:, off:off + n], b.ap[:, 0:n], ACT.Identity,
                                                  bias=vec("ml_gate_b")))
                        b.free = [t]
                        t_gate.append(t)

                    project("ml_g", 0, streams, gate)
                    one8 = TMP[:, 0, :]
                    t_dir = []
                    t_gf = []
                    VE.wait(t_gate)
                    for d in range(2):
                        rows = slice(32 * d, 32 * d + 8)
                        t_i = VE.done(ve.tensor_copy(G[rows, :], GATE[64 * d:64 * d + 8, :]))
                        t_f = VE.done(ve.tensor_copy(F[rows, :], GATE[64 * d + 32:64 * d + 40, :]))
                        t_gf.append((t_i, t_f))
                    W = RS
                    wt = [rs_free.get(0), rs_free.get(NL)]
                    t_col = [None]

                    def decay():
                        for d in range(2):
                            rows = slice(32 * d, 32 * d + 8)
                            SC.wait(t_gf[d][1], wt)
                            a = W[rows, :]
                            t = SC.done(sc.activation(a, F[rows, :], ACT.Abs))
                            SC.wait(t)
                            t = SC.done(sc.activation(a, a, ACT.Exp, scale=-1.0))
                            SC.wait(t)
                            t = SC.done(sc.activation(a, a, ACT.Ln, bias=1.0))
                            yield
                            VE.wait(t, t_gf[d][0], t_gf[d][1])
                            t = VE.done(ve.scalar_tensor_tensor(out=F[rows, :], in0=F[rows, :], scalar=0.0, in1=a,
                                                                op0=ALU.min, op1=ALU.subtract))
                            rs_free[0] = rs_free[NL] = t
                            VE.wait(t)
                            o8 = tmp.take()
                            VE.wait(o8.free)
                            o = o8.ap[rows, :]
                            t = VE.done(ve.memset(o, 1.0))
                            VE.wait(t)
                            f0, f1 = F[rows, 0:NC], F[rows, NC:NT]
                            g1, mm = G[rows, NC:NT], M[rows, :]
                            if d == 1:
                                f0, f1, g1, mm = f0[:, ::-1], f1[:, ::-1], g1[:, ::-1], mm[:, ::-1]
                            end = F[rows, NC - 1:NC] if d == 0 else F[rows, 0:1]
                            yield
                            t = VE.done(ve.tensor_tensor_scan(f0, o[:, 0:NC], f0, 0.0, ALU.mult, ALU.add))
                            VE.wait(t)
                            yield
                            t = VE.done(ve.tensor_tensor_scan(f1, o, f1, end, ALU.mult, ALU.add))
                            o8.free = [t]
                            VE.wait(t)
                            yield
                            t = VE.done(ve.tensor_tensor(G[rows, :], G[rows, :], F[rows, :], ALU.subtract))
                            VE.wait(t)
                            mx = SM[rows, 16:17]
                            t = VE.done(ve.tensor_reduce(mx, G[rows, 0:NC], AX.X, ALU.max))
                            VE.wait(t)
                            t = VE.done(ve.tensor_scalar(mx, mx, 0.0, None, ALU.max))
                            VE.wait(t)
                            yield
                            t = VE.done(ve.tensor_tensor_scan(mm, g1, g1, mx, ALU.max, ALU.max))
                            VE.wait(t)
                            yield
                            t = VE.done(ve.tensor_tensor(F[rows, NC:NT], F[rows, NC:NT], M[rows, :], ALU.add))
                            t2 = VE.done(ve.tensor_scalar(M[rows, :], M[rows, :], -1.0, None, ALU.mult))
                            SC.wait(t)
                            t = SC.done(sc.activation(F[rows, NC:NT], F[rows, NC:NT], ACT.Exp, scale=-1.0))
                            t_dir.append([t, t2])
                        yield
                        for d in range(2):
                            rows = slice(32 * d, 32 * d + 8)
                            b = bank()
                            PE.wait(t_dir, b.free)
                            for q in range(4):
                                for w_, src in ((0, M[rows, q * 128:(q + 1) * 128]),
                                                (1, F[rows, NC + q * 128:NC + (q + 1) * 128])):
                                    c = (w_ * 4 + q) * 8
                                    ins = pe.matmul(b.ap[:, c:c + 8], src, ident[rows, 32 * d:32 * d + 8], start=True,
                                                    stop=True)
                            t = PE.done(ins)
                            VE.wait(t)
                            t_col[0] = VE.done(ve.tensor_copy(COL[:, d, :, :, :].rearrange("p b c d -> p (b c d)"),
                                                           b.ap[:, 0:64]))
                            b.free = [t_col[0]]

                    heads.append(decay())

                    t_qk = []
                    wo = VEC_AT["ml_conv_w"][0]
                    bo = VEC_AT["ml_conv_b"][0]
                    for m in range(8):
                        ts = []

                        def conv(si, b, t, m=m, ts=ts):
                            off, n = spans[si]
                            dst = QQ[:, m, :] if m < 4 else KK[:, m - 4, off:off + n]
                            gv = b.ap[:, 0:n]
                            SC.wait(t)
                            t = SC.done(sc.activation(dst, gv, ACT.Identity, bias=VEC[:, bo + m:bo + m + 1],
                                                      scale=VEC[:, wo + 8 + m:wo + 9 + m]))
                            VE.wait(t)
                            t = VE.done(ve.scalar_tensor_tensor(out=dst[:, 1:n], in0=gv[:, 0:n - 1],
                                                                scalar=VEC[:, wo + m:wo + m + 1], in1=dst[:, 1:n],
                                                                op0=ALU.mult, op1=ALU.add))
                            VE.wait(t)
                            t = VE.done(ve.scalar_tensor_tensor(out=dst[:, 0:n - 1], in0=gv[:, 1:n],
                                                                scalar=VEC[:, wo + 16 + m:wo + 17 + m],
                                                                in1=dst[:, 0:n - 1], op0=ALU.mult, op1=ALU.add))
                            b.free = [t]
                            SC.wait(t)
                            ts.append(SC.done(sc.activation(dst, dst, ACT.Silu)))

                        project("ml_qk", m, streams[0:1] if m < 4 else streams, conv)
                        t_qk.append(ts)
                    t_v = []

                    def keep_v(c, tb, b, t):
                        SC.wait(t)
                        t = SC.done(sc.activation(V[:, tb, 512 * c:512 * c + 512], b.ap, ACT.Copy))
                        b.free = [t]
                        t_v.append(t)

                    def block(tb):
                        src, c = (HC, tb) if tb < 2 else (H, tb - 2)
                        return lambda k: src[:, k, c * 128:(c + 1) * 128]

                    token_rows("ml_v", 2, [block(tb) for tb in range(6)], keep_v)
                    t_o = []
                    for m in range(8):
                        def gate_o(si, b, t, m=m):
                            SC.wait(t)
                            t = SC.done(sc.activation(O[:, m, :], b.ap, ACT.Sigmoid))
                            b.free = [t]
                            t_o.append(t)

                        project("ml_o", m, streams[0:1], gate_o)
                    while heads:
                        advance()

                with ExitStack() as scope:
                    HT = alloc(scope, 4, 1024)
                    with ExitStack() as inner:
                        CM = alloc(inner, 1280)
                        GB = alloc(inner, 2, 2, NT)
                        MG = alloc(inner, 2, 2, NL)
                        prot = Rotor([Slot(alloc(inner, NT)[:, :]) for _ in range(3)])
                        drot = Rotor([Slot(alloc(inner, NT)[:, :]) for _ in range(2)])
                        trot = Rotor([Slot(alloc(inner, NT)[:, :]) for _ in range(2)])
                        free = t_o[-1]
                        VE.wait(free)
                        co = CONST_AT["mask_f"][0]
                        t_cm = fetch(CM[:, :], consts[:, co:co + 1280], free)
                        masks = [CM[:, 0:128], CM[:, 128:256]]
                        selm = CM[:, 256:1280].rearrange("p (h n) -> p h n", h=8)
                        gb_free = [[], []]
                        t_gb = {}

                        def spread(h):
                            k = h % 2
                            for d in range(2):
                                rows = slice(32 * d, 32 * d + 8)
                                ba, bb = turn_banks.take()
                                PE.wait(t_cm, t_dir, ba.free, bb.free)
                                pe.matmul(ba.ap[:, 0:NC], selm[rows, h, :], G[rows, 0:NC], start=True, stop=True)
                                t = PE.done(pe.matmul(bb.ap, selm[rows, h, :], G[rows, NC:NT], start=True, stop=True))
                                SC.wait(t, gb_free[k])
                                sc.activation(GB[:, k, d, 0:NC], ba.ap[:, 0:NC], ACT.Copy)
                                t = SC.done(sc.activation(GB[:, k, d, NC:NT], bb.ap, ACT.Copy))
                                ba.free = [t]
                                bb.free = [t]
                                VE.wait(t, gb_free[k])
                                t2 = VE.done(ve.tensor_tensor(
                                    MG[:, k, d, :].rearrange("p (b n) -> p b n", b=4),
                                    GB[:, k, d, NC:NT].rearrange("p (b n) -> p b n", b=4),
                                    masks[d].unsqueeze(1).broadcast_to([P, 4, 128]), ALU.add))
                                t_gb[(h, d)] = [t, t2]

                        t_ht = {}

                        def unit(h, q, d):
                            u = {}
                            rows = slice(64 * (h % 2), 64 * (h % 2) + 64)
                            key = (h, q)
                            blocks = [0, 1] + (list(range(2, 3 + q)) if d == 0 else list(range(2 + q, 6)))

                            def scores():
                                if d == 1:
                                    return
                                if q == 0:
                                    spread(h)
                                sb_ = score_banks.take()
                                t_ht[key] = {"b": sb_}
                                PE.wait(t_qk[h // 2], t_qk[4 + h // 2], sb_[0].free, sb_[1].free)
                                l = QQ[rows, h // 2, q * 128:(q + 1) * 128]
                                pe.matmul(sb_[0].ap[:, 0:384], l, KK[rows, h // 2, 0:384], start=True, stop=True)
                                t_ht[key]["t"] = PE.done(pe.matmul(sb_[1].ap[:, 0:384], l, KK[rows, h // 2, 384:768],
                                                                   start=True, stop=True))

                            def weights_():
                                st = t_ht[key]
                                dd, p, m = drot.take(), prot.take(), small.take()
                                u["p"], u["m"] = p, m
                                bias = COL[:, d, 0, q, h:h + 1]
                                g = GB[:, h % 2, d, :]
                                SC.wait(t_gb[(h, d)], t_col[0], dd.free)
                                c = NC + 128 * q
                                plain = [(0, c)] if d == 0 else [(0, NC)] + ([(c + 128, NT)] if q < 3 else [])
                                for a0, a1 in plain:
                                    sc.activation(dd.ap[:, a0:a1], g[:, a0:a1], ACT.Exp, bias=bias)
                                tD = SC.done(sc.activation(dd.ap[:, c:c + 128],
                                                           MG[:, h % 2, d, q * 128:(q + 1) * 128], ACT.Exp, bias=bias))
                                gb_free[h % 2] = [tD]
                                if d == 0:
                                    parts = [(0, 0, 384)] + ([(1, 0, 128 * q)] if q else [])
                                elif q == 0:
                                    parts = [(0, 0, 384), (1, 0, 384)]
                                else:
                                    parts = [(0, 0, 256), (1, 128 * (q - 1), 384)]
                                VE.wait(tD, st["t"], p.free, m.free)
                                for i, (bk, a0, a1) in enumerate(parts):
                                    o = 384 * bk
                                    t = VE.done(ve.scalar_tensor_tensor(
                                        out=p.ap[:, o + a0:o + a1], in0=st["b"][bk].ap[:, a0:a1], scalar=0.125,
                                        in1=dd.ap[:, o + a0:o + a1], op0=ALU.mult, op1=ALU.mult,
                                        accum_out=m.ap[:, i:i + 1]))
                                dd.free = [t]
                                u["t"] = t
                                if d == 1:
                                    st["b"][0].free = [t]
                                    st["b"][1].free = [t]
                                a = m.ap
                                if len(parts) == 2:
                                    VE.wait(t)
                                    t = VE.done(ve.tensor_tensor(a[:, 0:1], a[:, 0:1], a[:, 1:2], ALU.add))
                                VE.wait(t)
                                t = VE.done(ve.scalar_tensor_tensor(out=a[:, 2:3], in0=a[:, 0:1], scalar=-1.0,
                                                                    in1=a[:, 0:1], op0=ALU.mult, op1=ALU.max))
                                VE.wait(t)
                                t = VE.done(ve.tensor_tensor(a[:, 2:3], a[:, 2:3], COL[:, d, 1, q, h:h + 1], ALU.max))
                                VE.wait(t)
                                u["tr"] = VE.done(ve.reciprocal(a[:, 3:4], a[:, 2:3]))

                            def turn_():
                                u["o"], u["to"] = turn(u["p"], blocks, u["t"], trot)

                            def values():
                                b = value_banks.take()
                                PE.wait(u["to"], b.free, t_v)
                                n = len(blocks)
                                for i, kb in enumerate(blocks):
                                    ins = pe.matmul(b.ap[:, 0:128], u["o"].ap[:, i * 128:(i + 1) * 128],
                                                    V[:, kb, h * 128:(h + 1) * 128], start=(i == 0), stop=(i == n - 1))
                                t = PE.done(ins)
                                u["o"].free = [t]
                                dst = HT[:, q, h * 128:(h + 1) * 128]
                                VE.wait(t, u["tr"])
                                if d == 0:
                                    t = VE.done(ve.tensor_scalar(dst, b.ap[:, 0:128], u["m"].ap[:, 3:4], None, ALU.mult))
                                else:
                                    VE.wait(t_ht[key]["h"])
                                    t = VE.done(ve.scalar_tensor_tensor(out=dst, in0=b.ap[:, 0:128],
                                                                        scalar=u["m"].ap[:, 3:4], in1=dst,
                                                                        op0=ALU.mult, op1=ALU.add))
                                t_ht[key]["h"] = t
                                b.free = [t]
                                u["m"].free = [t]
                                if d == 1:
                                    t_ht[key]["ss"] = square_sum(dst, 8 * q + h, t)

                            return dict(scores=scores, weights=weights_, turn=turn_, values=values)

                        run_units([unit(h, q, d) for h in range(8) for q in range(4) for d in range(2)])
                    toks = scale_rows(HT, 128.0, EPS, [x["ss"] for x in t_ht.values()])
                    MX = alloc_pair(scope, KT, NL)

                    def use(k, b, n, t):
                        s = tmp.take()
                        VE.wait(t, s.free, t_o[k])
                        t = VE.done(ve.scalar_tensor_tensor(out=s.ap, in0=b.ap, scalar=vec("ml_out_g", k),
                                                            in1=O[:, k, :], op0=ALU.mult, op1=ALU.mult))
                        b.free = [t]
                        return pair_from(s, s.ap, MX.hi[:, k, :], MX.lo[:, k, :], t)

                    t = turn_mix(lambda tb: HT[:, tb, :], [0, 1, 2, 3], None, toks, use)
                    t_end = project_out("ml_out", [MX], t, lambda m, si: mod(1, 2, m, 0), t_mod[(1, 2)])
                    state["arena_free"] = [t_end]

        def square_sum(v, col, t):
            s = tmp.take()
            SC.wait(t, s.free)
            t = SC.done(sc.activation(s.ap[:, 0:128], v, ACT.Square, accum_out=SM[:, 32 + col:33 + col]))
            s.free = [t]
            return t

        def scale_rows(HT, count, eps, toks):
            c = SM[:, 32:64]
            SC.wait(toks)
            t = SC.done(sc.activation(c, c, ACT.Sqrt, bias=eps_ap(eps), scale=1.0 / count))
            VE.wait(t)
            t = VE.done(ve.reciprocal(c, c))
            VE.wait(t)
            SC.wait(t)
            out = []
            for q in range(4):
                for h in range(8):
                    v = HT[:, q, h * 128:(h + 1) * 128]
                    r = SM[:, 32 + 8 * q + h:33 + 8 * q + h]
                    if h % 2:
                        out.append(VE.done(ve.tensor_scalar(v, v, r, None, ALU.mult)))
                    else:
                        out.append(SC.done(sc.activation(v, v, ACT.Copy, scale=r)))
            return out

        def recurrent():
            with ExitStack() as base:
                GATE = alloc(base, 8, NL)
                REC = alloc(base, 8, NL)
                BX = alloc(base, 8, NL)
                AA = alloc(base, 8, NL)
                MU = alloc(base, 8, NL)
                wo = VEC_AT["rec_conv_w_2"][0]
                bo = VEC_AT["rec_conv_b_2"][0]
                t_gate, t_ri, t_a, t_m2, t_b, t_h = [], [], [], [], [], []
                with ExitStack() as scope:
                    H = alloc_pair(scope, KT, NL)
                    GW = alloc(scope, 2, 1024)
                    t_gw = []
                    for g in range(2):
                        src = weights["rec_g"][g * P * 1024:(g + 1) * P * 1024].rearrange("(p f) -> p f", p=P)
                        t_gw.append(fetch(GW[:, g, :], src, state["arena_free"]))
                    th = norm_main(H, None, second_gain("mix_norm_2"), None, [])[0]
                    lo = VEC_AT["rec_lambda_2"][0]
                    lam = VEC[:, lo:lo + 8]
                    z, u, v, acc = SM[:, 32:40], SM[:, 40:48], SM[:, 48:56], SM[:, 56:64]
                    t = SC.done(sc.activation(z, lam, ACT.Abs))
                    SC.wait(t)
                    t = SC.done(sc.activation(z, z, ACT.Exp, scale=-1.0))

                    def step(ins):
                        t = VE.done(ins)
                        VE.wait(t)
                        return t

                    VE.wait(t)
                    step(ve.tensor_scalar(u, z, 2.0, None, ALU.add))
                    step(ve.reciprocal(u, u))
                    step(ve.tensor_tensor(u, z, u, ALU.mult))
                    step(ve.tensor_tensor(v, u, u, ALU.mult))
                    step(ve.memset(acc, 1.0 / 19))
                    for q in range(8, -1, -1):
                        step(ve.tensor_tensor(acc, acc, v, ALU.mult))
                        step(ve.tensor_scalar(acc, acc, 1.0 / (2 * q + 1), None, ALU.add))
                    step(ve.tensor_tensor(acc, acc, u, ALU.mult))
                    step(ve.tensor_scalar(u, lam, -1.0, 0.0, ALU.mult, ALU.max))
                    step(ve.scalar_tensor_tensor(out=acc, in0=acc, scalar=2.0, in1=u, op0=ALU.mult, op1=ALU.add))
                    step(ve.tensor_scalar(acc, acc, 8.0, None, ALU.mult))
                    t_sp = step(ve.tensor_scalar(u, acc, -1.0, None, ALU.mult))
                    SC.wait(t_sp)

                    def channel(m, b, t):
                        r = REC[:, m, :]
                        SC.wait(t)
                        t = SC.done(sc.activation(r, b.ap, ACT.Identity, bias=VEC[:, bo + m:bo + m + 1],
                                                  scale=VEC[:, wo + 24 + m:wo + 25 + m]))
                        for q in range(3):
                            sh = 3 - q
                            VE.wait(t)
                            t = VE.done(ve.scalar_tensor_tensor(out=r[:, sh:NL], in0=b.ap[:, 0:NL - sh],
                                                                scalar=VEC[:, wo + 8 * q + m:wo + 8 * q + m + 1],
                                                                in1=r[:, sh:NL], op0=ALU.mult, op1=ALU.add))
                        b.free = [t]
                        t_rec = t
                        yield
                        both = []
                        for g, dst, name in ((0, AA, "rec_b_a_2"), (1, BX, "rec_b_x_2")):
                            b = bank()
                            t = mm_group(b.ap, [(GW[:, g, 128 * m:128 * m + 128], r)], [t_gw[g], t_rec, b.free])
                            SC.wait(t)
                            t = SC.done(sc.activation(dst[:, m, :], b.ap, ACT.Sigmoid, bias=vec(name, m)))
                            b.free = [t]
                            both.append(t)
                        GP.wait(both[1], t_rec)
                        t_b.append(GP.done(gp.tensor_tensor(BX[:, m, :], BX[:, m, :], r, ALU.mult)))
                        SC.wait(both[0])
                        tT = SC.done(sc.activation(MU[:, m, :], AA[:, m, :], ACT.Tanh, scale=acc[:, m:m + 1]))
                        t_a.append(SC.done(sc.activation(AA[:, m, :], AA[:, m, :], ACT.Exp, scale=u[:, m:m + 1])))
                        yield
                        q = tmp.take()
                        VE.wait(tT, q.free)
                        step(ve.tensor_scalar(q.ap, MU[:, m, :], 1.0, None, ALU.add))
                        step(ve.reciprocal(q.ap, q.ap))
                        t = VE.done(ve.scalar_tensor_tensor(out=MU[:, m, :], in0=MU[:, m, :], scalar=2.0, in1=q.ap,
                                                            op0=ALU.mult, op1=ALU.mult))
                        q.free = [t]
                        t_m2.append(t)

                    def scan(m):
                        VE.wait(t_mu, t_b[m])
                        t = VE.done(ve.tensor_tensor(BX[:, m, :], BX[:, m, :], MU[:, m, :], ALU.mult))
                        VE.wait(t, t_a[m])
                        t_h.append(VE.done(ve.tensor_tensor_scan(REC[:, m, :], AA[:, m, :], BX[:, m, :], 0.0, ALU.mult,
                                                                 ALU.add)))

                    for m in range(8):
                        project("rec_in", 8 + m, [(H, NL, th)], lambda si, b, t, m=m: channel(m, b, t))

                    def gelu(m, b, t):
                        SC.wait(t)
                        t = SC.done(sc.activation(GATE[:, m, :], b.ap, ACT.Gelu_apprx_tanh))
                        b.free = [t]
                        t_gate.append(t)

                    for m in range(8):
                        project("rec_in", m, [(H, NL, th)], lambda si, b, t, m=m: gelu(m, b, t))
                        if m == 3:
                            while heads:
                                advance()
                            SC.wait(t_m2)
                            t_mu = SC.done(sc.activation(MU[:, :, :], MU[:, :, :], ACT.Sqrt))
                        if m > 3:
                            scan(2 * (m - 4))
                            scan(2 * (m - 4) + 1)
                with ExitStack() as scope:
                    MX = alloc_pair(scope, KT, NL)
                    t_out = []
                    for m in range(8):
                        VE.wait(t_h[m], t_gate[m])
                        t = VE.done(ve.tensor_tensor(GATE[:, m, :], GATE[:, m, :], REC[:, m, :], ALU.mult))
                        t_out.append(pair_from(Slot(None), GATE[:, m, :], MX.hi[:, m, :], MX.lo[:, m, :], t))
                    t_end = project_out("rec_out", [MX], t_out, lambda m, si: 1.0, None)
                    state["arena_free"] = [t_end]

        shared = {}

        def qk_tile(b, tb, gain, dst, R2, rot2, t_r2, put):
            s = tmp.take()
            SC.wait(tb, s.free)
            t = SC.done(sc.activation(s.ap, b.ap, ACT.Square))
            yield
            b2 = bank()
            tq = mm_group(b2.ap, [(bones, s.ap)], [t, b2.free])
            s.free = [tq]
            r = tmp.take()
            VE.wait(r.free)
            t = rstd_of(b2, slice(0, P), NL, 64, EPS, r.ap, tq)
            q = tmp.take()
            VE.wait(t, q.free, tb)
            t = VE.done(ve.scalar_tensor_tensor(out=q.ap, in0=b.ap, scalar=gain, in1=r.ap, op0=ALU.mult,
                                                op1=ALU.mult))
            r.free = [t]
            b.free = [t]
            yield
            b3 = bank()
            tr = mm_group(b3.ap, [(rot2, q.ap)], [t, t_r2, b3.free])
            u = tmp.take()
            VE.wait(tr, u.free, t_r2)
            t1 = VE.done(ve.tensor_tensor(u.ap, b3.ap, R2[:, 512:1024], ALU.mult))
            b3.free = [t1]
            t2 = VE.done(ve.tensor_tensor(q.ap, q.ap, R2[:, 0:512], ALU.mult))
            VE.wait(t1, t2)
            t = VE.done(ve.tensor_tensor(dst, q.ap, u.ap, ALU.add))
            q.free = [t]
            u.free = [t]
            put(t)

        def rope2(scope, free):
            R2 = alloc(scope, 1024)
            rot = alloc(scope, 128)
            return R2, rot[:, :], [fetch(R2[:, :], const("rope_2"), free), fetch(rot[:, :], const("rot_2"), free)]

        def shared_kv(KS, VS):
            with ExitStack() as scope:
                H = alloc_pair(scope, KT, NL)
                R2, rot2, t_r2 = rope2(scope, state["arena_free"])
                th = norm_main(H, None, second_gain("kv_norm_2"), None, [])[0]
                t_k = [None] * 8
                for h in range(8):
                    def use(si, b, t, h=h):
                        return qk_tile(b, t, vec("k_norm_2"), KS[:, h, :], R2, rot2, t_r2,
                                       lambda t: t_k.__setitem__(h, t))

                    project("wk", h, [(H, NL, th)], use)
                advance()
                t_v = []

                def keep_v(c, tb, b, t):
                    SC.wait(t)
                    t = SC.done(sc.activation(VS[:, tb, 512 * c:512 * c + 512], b.ap, ACT.Copy))
                    b.free = [t]
                    t_v.append(t)

                token_rows("wv", 2, [lambda k, tb=tb: H[:, k, tb * 128:(tb + 1) * 128] for tb in range(4)], keep_v)
                shared.update(k=t_k, v=t_v)
                state["arena_free"] = [t_v[-1], t_k[7]]

        def diff_attention(KS, VS):
            with ExitStack() as base:
                Q = alloc(base, 8, NL)
                HT = alloc(base, 4, 1024)
                LM = SM[:, 64:72]
                cols = [VEC_AT[x][0] for x in ("lambda_q1_2", "lambda_q2_2", "lambda_k1_2", "lambda_k2_2")]
                t = VE.done(ve.tensor_tensor(LM[0:64, 0:2], VEC[0:64, cols[0]:cols[0] + 2],
                                             VEC[0:64, cols[2]:cols[2] + 2], ALU.mult))
                b = bank()
                t = mm_group(b.ap[:, 0:2], [(ones[0:64, :], LM[0:64, 0:2])], [t, b.free])
                SC.wait(t)
                t = SC.done(sc.activation(LM[:, 2:4], b.ap[:, 0:2], ACT.Exp))
                b.free = [t]
                VE.wait(t)
                t = VE.done(ve.tensor_tensor(LM[:, 4:5], LM[:, 3:4], LM[:, 2:3], ALU.subtract))
                VE.wait(t)
                t = VE.done(ve.tensor_scalar(LM[:, 4:5], LM[:, 4:5], -LAMBDA_INIT, None, ALU.add))
                t2 = VE.done(ve.tensor_scalar(LM[:, 5:6], vec("q_norm_2"), 0.125, None, ALU.mult))
                t3 = VE.done(ve.tensor_scalar(LM[:, 6:7], vec("sub_norm_2"), 1.0 - LAMBDA_INIT, None, ALU.mult))
                VE.wait(t, t2, t3)
                SC.wait(t3)
                neg_lam, q_gain, o_gain = LM[:, 4:5], LM[:, 5:6], LM[:, 6:7]
                t_q = [None] * 8
                with ExitStack() as scope:
                    H = alloc_pair(scope, KT, NL)
                    R2, rot2, t_r2 = rope2(scope, state["arena_free"])
                    th = norm_main(H, None, second_gain("mix_norm_2", 8), None, [])[0]
                    for h in range(8):
                        def use(si, b, t, h=h):
                            return qk_tile(b, t, q_gain, Q[:, h, :], R2, rot2, t_r2,
                                           lambda t: t_q.__setitem__(h, t))

                        project("wq", h, [(H, NL, th)], use)
                    while heads:
                        advance()
                t_ht = {}
                with ExitStack() as scope:
                    prot = Rotor([Slot(alloc(scope, NL)[:, :]) for _ in range(3)])
                    trot = Rotor([Slot(alloc(scope, NT)[:, :]) for _ in range(3)])
                    VE.wait(t_q[7])
                    SC.wait(t_q[7])
                    GP.wait(t_q[7])

                    def finish_in(h, q, comp):
                        dst = HT[:, q, h * 128:(h + 1) * 128]

                        def finish(b, m, slot):
                            if comp == 0:
                                t = VE.done(ve.tensor_scalar(dst, b.ap[:, 0:128], m[:, 3:4], None, ALU.mult))
                                t_ht[(h, q)] = t
                                b.free = [t]
                                slot.free = [t]
                                return
                            t = VE.done(ve.tensor_scalar(m[:, 4:5], m[:, 3:4], neg_lam, None, ALU.mult))
                            VE.wait(t, t_ht[(h, q)])
                            t = VE.done(ve.scalar_tensor_tensor(out=dst, in0=b.ap[:, 0:128], scalar=m[:, 4:5],
                                                                in1=dst, op0=ALU.mult, op1=ALU.add))
                            b.free = [t]
                            slot.free = [t]
                            t_ht[(h, q)] = square_sum(dst, 8 * q + h, t)
                        return finish

                    units = []
                    for h in range(8):
                        for q in range(4):
                            for comp in range(2):
                                rows = slice(64 * comp, 64 * comp + 64)
                                units.append(softmax_unit(
                                    Q[rows, h, q * 128:(q + 1) * 128], KS[rows, h, :], 128 * (q + 1), 1.0, True,
                                    lambda kb, h=h: VS[:, kb, h * 128:(h + 1) * 128], [t_q[h], shared["k"][h]],
                                    shared["v"], prot, trot, finish_in(h, q, comp)))
                    run_units(units)
                toks = scale_rows(HT, 128.0, SUB_EPS, list(t_ht.values()))
                MX = alloc_pair(base, KT, NL)

                def use(k, b, n, t):
                    hi, lo = MX.hi[:, k, :], MX.lo[:, k, :]
                    SC.wait(t)
                    t1 = SC.done(sc.activation(hi, b.ap, ACT.Copy, scale=o_gain))
                    VE.wait(t1)
                    t2 = VE.done(ve.scalar_tensor_tensor(out=lo, in0=b.ap, scalar=o_gain, in1=hi.bitcast(F32),
                                                         op0=ALU.mult, op1=ALU.subtract))
                    b.free = [t2]
                    return t2

                t = turn_mix(lambda tb: HT[:, tb, :], [0, 1, 2, 3], None, toks, use)
                t_end = project_out("wo", [MX], t, lambda m, si: 1.0, None)
                state["arena_free"] = [t_end]

        early = ExitStack()
        ROWS = alloc(early, NL)
        for i in range(16):
            ada_chunk(0, i)
        ada_end()
        side.extend([(0, i) for i in range(16, 48)])
        ada_t = alloc(early, 2, 1024)
        ada_ring = Rotor([Slot(ada_t[:, i, :]) for i in range(2)])
        ada_sem = [sem(f"s_a{i}") for i in range(3)]
        even_mixer()
        side.extend([(1, i) for i in range(48)])
        modulated_ffn("up0", "down0", 0, True)
        run_side(99)
        state["arena_free"] += [ada_ring.slots[i].free[0] for i in range(2)]
        state["arena_free"] += [row_read[0]]
        early.close()
        bank_turns[0] = 8
        odd_mixer()
        modulated_ffn("up1", "down1", 1, False)
        half_ffn("s_up10", "s_down10", second_gain("ffn1_norm_2"))
        recurrent()
        half_ffn("s_up20", "s_down20", second_gain("ffn2_norm_2"))
        with ExitStack() as kept:
            KS = alloc(kept, 8, NL)
            VS = alloc(kept, 4, 1024)
            shared_kv(KS, VS)
            half_ffn("s_up11", "s_down11", second_gain("ffn1_norm_2", 8))
            diff_attention(KS, VS)
        half_ffn("s_up21", "s_down21", second_gain("ffn2_norm_2", 8))

        s_out = sem("s_out")
        out = outT.rearrange("(k p) t -> p k t", p=P)
        for m in range(KT):
            sp_wait(state["x"][m])
            nc.sync.dma_start(out[:, m, :], X[:, m, :]).then_inc(s_out, 16)
        nc.sync.wait_ge(s_out, 16 * KT)


def _columns(w, n):
    k = w.shape[0] // P
    return w.reshape(k, P, w.shape[1] // n, n).transpose(2, 1, 0, 3)


def _up(gate, val):
    return np.stack([_columns(gate, 128), _columns(val, 128)], 1)


def _down(w):
    t = w.reshape(FT, P, 8, 128).transpose(2, 1, 0, 3)
    return np.concatenate([t[m, :, a:b].reshape(-1) for a, b in GROUPS for m in range(8)])


def _rows(w):
    return w.reshape(4, 2, P, w.shape[1] // 512, 512).transpose(3, 0, 2, 1, 4)


def _layout(i):
    w = {}
    for l in range(2):
        w[f"ada{l}"] = _rows(i["ada_w"][l])
        w[f"up{l}"] = _up(i["ffn_w_up"][l][:, :2816], i["ffn_w_up"][l][:, 2816:])
        w[f"down{l}"] = _down(i["ffn_w_down"][l])
        for f in (1, 2):
            w[f"s_up{f}{l}"] = _up(i[f"ffn{f}_w_gate_2"][l], i[f"ffn{f}_w_up_2"][l])
            w[f"s_down{f}{l}"] = _down(i[f"ffn{f}_w_down_2"][l])
    a = i["att_w_in"][0]
    kr = np.zeros((D, 128), np.float32)
    kr[:, 64:96] = a[:, 640:672]
    w["att_in"] = _columns(np.concatenate([a[:, 0:640], kr, a[:, 672:1440]], 1), 128)
    w["qb"] = i["mla_w_qb"][0].reshape(3, P, 4, 2, 96).transpose(2, 1, 3, 0, 4)
    kv = i["mla_w_kvb"][0].reshape(2, P, 8, 128)
    w["kb"] = kv[..., :64].transpose(1, 2, 0, 3)
    w["vb"] = kv[..., 64:].transpose(1, 0, 2, 3)
    w["att_out"] = _columns(i["att_w_out"][0], 128)
    m = i["ml_w_in"][0]
    w["ml_qk"] = _columns(m[:, 0:1024], 128)
    w["ml_v"] = _rows(m[:, 1024:2048])
    w["ml_o"] = _columns(m[:, 2048:3072], 128)
    g = np.zeros((D, 4, 32), np.float32)
    g[:, :, 0:8] = m[:, 3072:3104].reshape(D, 4, 8)
    w["ml_g"] = _columns(g.reshape(D, 128), 128)
    w["ml_out"] = _columns(i["ml_w_out"][0], 128)
    w["rec_in"] = _columns(i["rec_w_in_2"][0], 128)
    w["rec_g"] = np.stack([i["rec_w_a_2"][0], i["rec_w_x_2"][0]]).transpose(0, 2, 1, 3)
    w["rec_out"] = _columns(i["rec_w_out_2"][0], 128)
    w["wk"] = _columns(i["w_k_2"], 128)
    w["wv"] = _rows(i["w_v_2"])
    w["wq"] = _columns(i["attn_w_q_2"][0], 128)
    w["wo"] = _columns(i["attn_w_o_2"][0], 128)
    w = {k: np.ascontiguousarray(v).reshape(-1) for k, v in w.items()}

    vecs = np.zeros((P, NVEC), np.float32)
    for name, (o, n) in VEC_AT.items():
        v = i[name]
        if name in ("mla_q_g", "mla_k_g", "lambda_q1_2", "lambda_q2_2", "lambda_k1_2", "lambda_k2_2"):
            v = v.reshape(-1)
            vecs[0:v.size, o] = v
        elif name in ("gqa_q_g", "gqa_k_g", "k_norm_2", "q_norm_2"):
            vecs[0:64, o] = v.reshape(-1)
            vecs[64:128, o] = v.reshape(-1)
        elif name == "ml_gate_b":
            for q in range(4):
                vecs[32 * q:32 * q + 8, o] = v.reshape(4, 8)[q]
        else:
            vecs[:, o:o + n] = v.reshape(n, P).T
    return w, vecs


def _rope_axial(dim):
    rows = NL // 64
    row = np.repeat(np.arange(rows), 64).astype(np.float32)
    col = np.tile(np.arange(64), rows).astype(np.float32)
    nf = dim // 4
    inv = np.float32(10000.0) ** (-np.arange(nf, dtype=np.float32) / np.float32(nf))
    a, b = row[:, None] * inv, col[:, None] * inv
    ang = np.concatenate([a, a, b, b], axis=-1)
    return np.cos(ang).T, np.sin(ang).T


def _constants():
    c = np.zeros((P, NCONST), np.float32)

    def put(name, v):
        o, n = CONST_AT[name]
        c[:v.shape[0], o:o + v.shape[1]] = v

    put("ident", np.eye(P, dtype=np.float32))
    put("ones", np.ones((P, P), np.float32))
    put("bones", np.kron(np.eye(2), np.ones((64, 64))))

    def quarter(d):
        q = d // 4
        r = np.zeros((d, d))
        for i in range(q):
            r[i, q + i] = -1
            r[q + i, i] = 1
            r[2 * q + i, 3 * q + i] = -1
            r[3 * q + i, 2 * q + i] = 1
        return r.T

    def half(d):
        q = d // 2
        r = np.zeros((d, d))
        for i in range(q):
            r[i, q + i] = -1
            r[q + i, i] = 1
        return r.T

    put("rot_g", np.kron(np.eye(2), quarter(64)))
    rm = np.zeros((P, P))
    rm[64:96, 64:96] = quarter(32)
    put("rot_m", rm)
    put("rot_2", np.kron(np.eye(2), half(64)))
    s, t = np.arange(P)[:, None], np.arange(P)[None, :]
    put("mask_f", np.where(t <= s, 0.0, -1e30))
    put("mask_b", np.where(t >= s, 0.0, -1e30))
    sel = np.zeros((P, 8, P))
    for h in range(8):
        sel[h, h] = 1
        sel[32 + h, h] = 1
    put("sel", sel.reshape(P, 1024))
    cm, sm = _rope_axial(32)
    rm = np.zeros((P, 1024))
    rm[64:96, 0:512], rm[64:96, 512:1024] = cm, sm
    put("rope_m", rm)
    cg, sg = _rope_axial(64)
    put("rope_g", np.concatenate([np.tile(cg, (2, 1)), np.tile(sg, (2, 1))], 1))
    pos = np.arange(NL, dtype=np.float32)
    inv = np.float32(10000.0) ** (-np.arange(0, 64, 2, dtype=np.float32) / np.float32(64))
    ang = pos[:, None] * inv[None, :]
    ang = np.concatenate([ang, ang], axis=-1)
    put("rope_2", np.concatenate([np.tile(np.cos(ang).T, (2, 1)), np.tile(np.sin(ang).T, (2, 1))], 1))
    return c


def _program(nc, arrays):
    def given(name):
        a = arrays[name]
        return nc.dram_tensor(name, list(a.shape), F32, kind="ExternalInput").ap()

    out = nc.dram_tensor("outT", [D, NL], F32, kind="ExternalOutput").ap()
    weights = {name: given("w_" + name) for name in CHUNKS}
    build(nc, given("xT"), given("ctxT"), given("vecs"), given("consts"), weights, out)


def _arrays(inputs):
    i = {k: np.asarray(v) for k, v in inputs.items()}
    w, vecs = _layout(i)
    arrays = {"w_" + k: v for k, v in w.items()}
    arrays["xT"] = np.ascontiguousarray(i["x"][0].T)
    arrays["ctxT"] = np.ascontiguousarray(i["ctx"][0].T)
    arrays["vecs"] = vecs
    arrays["consts"] = _constants()
    return arrays


def kernel(**inputs):
    import concourse.bacc as bacc
    from concourse.bass_utils import run_bass_kernel_spmd

    arrays = _arrays(inputs)
    nc = bacc.Bacc("TRN2", target_bir_lowering=False, num_devices=1)
    _program(nc, arrays)
    r = run_bass_kernel_spmd(nc, [arrays], core_ids=[0])
    return np.ascontiguousarray(r.results[0]["outT"].T).reshape(1, NL, D)
```
